# Optimizing a Trainium2 kernel written in Bass

```python
import math
import jax, jax.numpy as jnp
from jax import lax
import numpy as np

D_MODEL = 1024
BATCH = 1
SEQ = 256
DEPTH = 1

MIX_WIDTH = D_MODEL
FOURIER_WIDTH = D_MODEL // 4
FOURIER_GROUPS = 4
FOURIER_GROUP_DIM = FOURIER_WIDTH // FOURIER_GROUPS
ATTN_WIDTH = MIX_WIDTH - FOURIER_WIDTH
HEAD_DIM = 64
ATTN_HEADS = ATTN_WIDTH // HEAD_DIM
IN_PROJ_WIDTH = FOURIER_WIDTH + 3 * ATTN_WIDTH
DILATED_BRANCHES = ((128, 1), (512, 4), (2048, 16))
Q_BLOCK = 128
ROPE_THETA = 10000.0
NEG_INF = -1e30
PEER_N_KEYS = 128
PEER_N_EXPERTS = PEER_N_KEYS * PEER_N_KEYS
PEER_HEADS = 8
PEER_KEY_DIM = 128
PEER_HALF = PEER_KEY_DIM // 2
PEER_TOPK = 16
TOKEN_CHUNK = 128
LN_EPS = 1e-5
DEEPNORM_ALPHA = (2.0 * DEPTH) ** 0.25
DEEPNORM_BETA = (8.0 * DEPTH) ** -0.25

kernel_name = "hymba_fnet_longnet_peer_encoder"

def _normal(key, shape, std):
    return jax.random.normal(key, shape, jnp.float32) * std

def _normalize(x):
    xf = x.astype(jnp.float32)
    mu = jnp.mean(xf, axis=-1, keepdims=True)
    var = jnp.mean(jnp.square(xf - mu), axis=-1, keepdims=True)
    return ((xf - mu) * lax.rsqrt(var + LN_EPS)).astype(x.dtype)

def _layer_norm(x, gain, bias):
    return _normalize(x) * gain + bias

def _rope(t, positions):
    half = HEAD_DIM // 2
    inv_freq = ROPE_THETA ** (-jnp.arange(half, dtype=jnp.float32) / half)
    ang = positions.astype(jnp.float32)[..., None] * inv_freq
    cos = jnp.cos(ang)[:, :, None, :]
    sin = jnp.sin(ang)[:, :, None, :]
    tf = t.astype(jnp.float32)
    t1, t2 = tf[..., :half], tf[..., half:]
    out = jnp.concatenate([t1 * cos - t2 * sin, t2 * cos + t1 * sin], axis=-1)
    return out.astype(t.dtype)

def _fourier_mixer(f, w_fourier):
    b, s, _ = f.shape
    fg = f.reshape(b, s, FOURIER_GROUPS, FOURIER_GROUP_DIM).astype(jnp.float32)
    spec = jnp.fft.fft2(fg, axes=(1, 3), norm="ortho").real
    out = jnp.einsum('bsgc,gcd->bsgd', spec, w_fourier.astype(jnp.float32))
    return out.reshape(b, s, FOURIER_WIDTH).astype(f.dtype)

def _dilated_attention(q, k, v):
    b, h, s, dh = q.shape
    n_blocks = s // Q_BLOCK
    scale = HEAD_DIM ** -0.5

    def block(i):
        start = i * Q_BLOCK
        qb = lax.dynamic_slice_in_dim(q, start, Q_BLOCK, axis=2).astype(jnp.float32)
        pos = start + jnp.arange(Q_BLOCK, dtype=jnp.int32)
        lses, outs = [], []
        for window, dil in DILATED_BRANCHES:
            n_side = window // (2 * dil)
            offs = dil * jnp.arange(-n_side, n_side + 1, dtype=jnp.int32)
            idx = pos[:, None] + offs[None, :]
            valid = (idx >= 0) & (idx < s)
            idx = jnp.clip(idx, 0, s - 1)
            kg = jnp.take(k, idx, axis=2, mode='clip').astype(jnp.float32)
            vg = jnp.take(v, idx, axis=2, mode='clip').astype(jnp.float32)
            sc = jnp.einsum('bhqd,bhqkd->bhqk', qb, kg) * scale
            sc = jnp.where(valid, sc, NEG_INF)
            lse = jax.nn.logsumexp(sc, axis=-1)
            p = jnp.exp(sc - lse[..., None])
            outs.append(jnp.einsum('bhqk,bhqkd->bhqd', p, vg))
            lses.append(lse)
        w = jax.nn.softmax(jnp.stack(lses, axis=0), axis=0)
        return jnp.einsum('rbhq,rbhqd->bhqd', w, jnp.stack(outs, axis=0))

    out = lax.map(block, jnp.arange(n_blocks, dtype=jnp.int32))
    out = out.transpose(1, 0, 3, 2, 4).reshape(b, s, h * dh)
    return out.astype(q.dtype)

def _peer(h, w_peer_q, peer_subkeys, peer_u, peer_v):
    b, s, d = h.shape
    t = h.reshape(b * s, d)
    n_tok = b * s
    q = (t @ w_peer_q).reshape(n_tok, PEER_HEADS, 2, PEER_HALF).astype(jnp.float32)
    sub = jnp.einsum('thpc,hpkc->thpk', q, peer_subkeys.astype(jnp.float32))
    sv, si = lax.top_k(sub, PEER_TOPK)
    cand = (sv[:, :, 0, :, None] + sv[:, :, 1, None, :]).reshape(n_tok, PEER_HEADS, PEER_TOPK * PEER_TOPK)
    cid = (si[:, :, 0, :, None] * PEER_N_KEYS + si[:, :, 1, None, :]).reshape(n_tok, PEER_HEADS, PEER_TOPK * PEER_TOPK)
    top_v, top_pos = lax.top_k(cand, PEER_TOPK)
    expert_ids = jnp.take_along_axis(cid, top_pos, axis=-1)
    gates = jax.nn.softmax(top_v, axis=-1)
    ids = expert_ids.reshape(n_tok, PEER_HEADS * PEER_TOPK)
    gates = gates.reshape(n_tok, PEER_HEADS * PEER_TOPK)
    n_chunks = n_tok // TOKEN_CHUNK

    def chunk(args):
        tc, ic, gc = args
        ug = jnp.take(peer_u, ic, axis=0, mode='clip').astype(jnp.float32)
        act = jax.nn.gelu(jnp.einsum('ced,cd->ce', ug, tc.astype(jnp.float32)), approximate=False)
        vg = jnp.take(peer_v, ic, axis=0, mode='clip').astype(jnp.float32)
        return jnp.einsum('ce,ced->cd', gc * act, vg)

    y = lax.map(chunk, (t.reshape(n_chunks, TOKEN_CHUNK, d),
                        ids.reshape(n_chunks, TOKEN_CHUNK, -1),
                        gates.reshape(n_chunks, TOKEN_CHUNK, -1)))
    return y.reshape(b, s, d).astype(h.dtype)

def setup_inputs(seed: int = 0) -> dict:
    key = jax.random.key(seed)
    ks = jax.random.split(key, 18)
    d = D_MODEL
    x = _normal(ks[0], (BATCH, SEQ, d), 1.0)
    c = _normal(ks[1], (BATCH, d), 1.0)
    positions = (jnp.arange(SEQ, dtype=jnp.int32)[None, :]
                 + jax.random.randint(ks[2], (BATCH, 1), 0, 1024, dtype=jnp.int32))
    w_ada = _normal(ks[3], (DEPTH, d, 6 * d), 0.2 * d ** -0.5)
    b_ada = _normal(ks[4], (DEPTH, 6 * d), 0.01)
    w_in = _normal(ks[5], (DEPTH, d, IN_PROJ_WIDTH), d ** -0.5)
    b_in = _normal(ks[6], (DEPTH, IN_PROJ_WIDTH), 0.01)
    w_fourier = _normal(ks[7], (DEPTH, FOURIER_GROUPS, FOURIER_GROUP_DIM, FOURIER_GROUP_DIM), FOURIER_GROUP_DIM ** -0.5)
    w_out = _normal(ks[8], (DEPTH, MIX_WIDTH, d), DEEPNORM_BETA * MIX_WIDTH ** -0.5)
    b_out = _normal(ks[9], (DEPTH, d), 0.01)
    ln1_gain = 1.0 + _normal(ks[10], (DEPTH, d), 0.02)
    ln1_bias = _normal(ks[11], (DEPTH, d), 0.02)
    w_peer_q = _normal(ks[12], (DEPTH, d, PEER_HEADS * PEER_KEY_DIM), d ** -0.5)
    peer_subkeys = _normal(ks[13], (DEPTH, PEER_HEADS, 2, PEER_N_KEYS, PEER_HALF), PEER_HALF ** -0.5)
    peer_u = _normal(ks[14], (DEPTH, PEER_N_EXPERTS, d), d ** -0.5)
    peer_v = _normal(ks[15], (DEPTH, PEER_N_EXPERTS, d), DEEPNORM_BETA)
    ln2_gain = 1.0 + _normal(ks[16], (DEPTH, d), 0.02)
    ln2_bias = _normal(ks[17], (DEPTH, d), 0.02)
    return {"x": x, "c": c, "positions": positions,
            "w_ada": w_ada, "b_ada": b_ada, "w_in": w_in, "b_in": b_in,
            "w_fourier": w_fourier, "w_out": w_out, "b_out": b_out,
            "ln1_gain": ln1_gain, "ln1_bias": ln1_bias,
            "w_peer_q": w_peer_q, "peer_subkeys": peer_subkeys,
            "peer_u": peer_u, "peer_v": peer_v,
            "ln2_gain": ln2_gain, "ln2_bias": ln2_bias}

def reference(x, c, positions, w_ada, b_ada, w_in, b_in, w_fourier, w_out, b_out,
              ln1_gain, ln1_bias, w_peer_q, peer_subkeys, peer_u, peer_v,
              ln2_gain, ln2_bias):
    b, s, _ = x.shape
    cond = jax.nn.silu(c)
    for i in range(DEPTH):
        mod = (cond @ w_ada[i] + b_ada[i])[:, None, :]
        shift1, scale1, gate1, shift2, scale2, gate2 = jnp.split(mod, 6, axis=-1)

        h = _normalize(x) * (1.0 + scale1) + shift1
        proj = h @ w_in[i] + b_in[i]
        f_in = proj[..., :FOURIER_WIDTH]
        q, k, v = jnp.split(proj[..., FOURIER_WIDTH:], 3, axis=-1)
        q = _rope(q.reshape(b, s, ATTN_HEADS, HEAD_DIM), positions).transpose(0, 2, 1, 3)
        k = _rope(k.reshape(b, s, ATTN_HEADS, HEAD_DIM), positions).transpose(0, 2, 1, 3)
        v = v.reshape(b, s, ATTN_HEADS, HEAD_DIM).transpose(0, 2, 1, 3)
        mix_a = _fourier_mixer(f_in, w_fourier[i])
        mix_b = _dilated_attention(q, k, v)
        mix = jnp.concatenate([mix_a, mix_b], axis=-1) @ w_out[i] + b_out[i]
        x = _layer_norm(DEEPNORM_ALPHA * x + (1.0 + gate1) * mix, ln1_gain[i], ln1_bias[i])

        h = _normalize(x) * (1.0 + scale2) + shift2
        ffn = _peer(h, w_peer_q[i], peer_subkeys[i], peer_u[i], peer_v[i])
        x = _layer_norm(DEEPNORM_ALPHA * x + (1.0 + gate2) * ffn, ln2_gain[i], ln2_bias[i])
    return x


_drawn_inputs = setup_inputs


def setup_inputs(seed=0):
    import zlib

    import numpy as np

    out = dict(_drawn_inputs(seed))
    spreads = {}
    factors = {'b_in': 3.024, 'ln2_gain': 2.86, 'ln2_bias': 2.874}
    for name, (base, spread) in spreads.items():
        noise = np.random.default_rng([zlib.crc32(name.encode()), seed]).standard_normal(out[name].shape)
        drawn = base * np.exp(spread * noise) if base else spread * noise
        out[name] = __import__('jax').numpy.asarray(drawn.astype(out[name].dtype))
    for name, factor in factors.items():
        out[name] = (out[name] * factor).astype(out[name].dtype)
    return out
```

```python
import math
import numpy as np
import concourse.bass as bass
from concourse import mybir
from contextlib import ExitStack

D, S, T = 1024, 256, 2
KD = D // 128
FW, AW, NH, HD = 256, 768, 12, 64
NK, PH, KH, TOPK = 128, 8, 64, 16
ALPHA = 2.0 ** 0.25
EPS = 1e-5
NQ, QJ = 4, 32
BODY = 4
C_IOTA, C_BIAS, C_SEQ, C_CHAN, C_INVF, C_IOTA16, C_END = 128, 256, 768, 1792, 2048, 2080, 2304


def peer_encoder(nc, x, c, positions, w_ada, b_ada, w_in, b_in, w_fourier, w_out, b_out, ln1_gain,
                 ln1_bias, w_peer_q, peer_subkeys, peer_u, peer_v, ln2_gain, ln2_bias, table, out):
    f32, i32, u32 = mybir.dt.float32, mybir.dt.int32, mybir.dt.uint32
    ALU, ACT, AX = mybir.AluOpType, mybir.ActivationFunctionType, mybir.AxisListType
    ds = bass.ds

    x_v = x[0].rearrange("(t p) d -> p t d", p=128)
    out_v = out[0].rearrange("(t p) d -> p t d", p=128)
    pos_v = positions[0].rearrange("(t p) -> p t", p=128)
    ada_v = w_ada[0].rearrange("(k p) n -> p k n", p=128)
    win_v = w_in[0].rearrange("(k p) n -> p k n", p=128)
    wout_v = w_out[0].rearrange("(k p) n -> p k n", p=128)
    wpq_v = w_peer_q[0].rearrange("(k p) n -> p k n", p=128)
    u_v = peer_u[0].rearrange("(i j) d -> i (j d)", i=128)
    v_v = peer_v[0].rearrange("(i j) d -> i (j d)", i=128)
    CHUNKS = [ada_v[:, :, 0:D], ada_v[:, :, D:2 * D], win_v[:, :, 0:1024], win_v[:, :, 1024:2048],
              win_v[:, :, 2048:2560], ada_v[:, :, 2 * D:3 * D], ada_v[:, :, 3 * D:4 * D],
              ada_v[:, :, 4 * D:5 * D], wout_v, wpq_v, ada_v[:, :, 5 * D:6 * D]]
    SH1, SC1, WA, WB, WC, GT1, SH2, SC2, WO, WPQ, GT2 = range(11)
    NSLOT = 3

    with ExitStack() as ctx:
        def sb(name, n, dt=f32):
            return ctx.enter_context(nc.sbuf_tensor(name, [128, n], dt))

        def sem(name):
            return ctx.enter_context(nc.semaphore(name))

        big = sb("big", NSLOT * 8192)
        work = sb("work", 15360)
        const = sb("const", C_END)
        xs = sb("xs", T * D)
        hTs = sb("hTs", KD * S)
        uring = sb("uring", 4 * D)
        g1s = sb("g1s", D)
        g2s = sb("g2s", D)
        cols = sb("cols", 58)
        csil = sb("csil", 8)
        modc = sb("modc", 32)
        pos_i = sb("pos_i", T, i32)
        pos_f = sb("pos_f", T)
        stat = sb("stat", 2 * 6 + 2 + 2)
        rmax = sb("rmax", 2 * 4)
        rsum = sb("rsum", 2 * 4)

        ident = const[:, 0:128]
        iota = const[:, C_IOTA:C_IOTA + 128]
        bias_c = const[:, C_BIAS:C_SEQ].rearrange("p (q k) -> p q k", q=2)
        seq_c = const[:, C_SEQ:C_CHAN].rearrange("p (c k t) -> p c k t", c=2, k=2)
        chan_c = const[:, C_CHAN:C_INVF].rearrange("p (c n) -> p c n", c=2)
        invf = const[:, C_INVF:C_IOTA16]
        x3 = xs[:, :].rearrange("p (t d) -> p t d", t=T)
        hT = hTs[:, :].rearrange("p (k t) -> p k t", k=KD)
        slot3 = [big[:, s * 8192:(s + 1) * 8192].rearrange("p (k n) -> p k n", k=KD) for s in range(NSLOT)]
        wc3 = big[:, (WC % NSLOT) * 8192:(WC % NSLOT) * 8192 + 4096].rearrange("p (k n) -> p k n", k=KD)
        bin_row, bout_row = work[:, 9728:12032], work[:, 12032:13056]
        gain1, bias1 = work[:, 13056:14080], work[:, 14080:15104]
        rope_cs = work[:, 15104:15232].rearrange("p (c t f) -> p c t f", c=2, t=T)
        rope_w = work[:, 15232:15360].rearrange("p (a t f) -> p a t f", a=2, t=T)
        hn = work[:, 0:2048].rearrange("p (t d) -> p t d", t=T)
        qkv = work[:, 0:4608].rearrange("p (t n) -> p t n", t=T)
        qkT = work[:, 4608:7680].rearrange("p (n t) -> p n t", n=12)
        mixT = work[:, 7680:9728].rearrange("p (k t) -> p k t", k=KD)
        rtmp = work[:, 8192:9728].rearrange("p (a n f) -> p a n f", a=2, f=32)
        prob = work[:, 9728:10752].rearrange("p (b q k) -> p b q k", b=2, q=2)
        probT = work[:, 10752:11776].rearrange("p (b k q) -> p b k q", b=2, k=2)
        fT = uring[:, 0:512].rearrange("p (n t) -> p n t", n=2)
        fw = uring[:, 512:1536].rearrange("p (s n c m) -> p s n c m", s=2, n=2, c=2)
        wfd = uring[:, 1536:1792].rearrange("p (n m) -> p n m", n=2)
        wcs = uring[:, 1792:2304].rearrange("p (n c m) -> p n c m", n=2, c=2)
        rows = uring[0:58, 2304:2432]
        csilB = uring[:, 3072:4096].rearrange("p (k m) -> p k m", k=KD)
        vring = work[:, 0:4096]
        sub = work[:, 0:4096].rearrange("p (t s h k) -> p t s h k", t=T, s=2, h=PH)
        OI = work[:, 4096:6144].rearrange("p (b u i) -> p b u i", b=2, u=8)
        OJ = work[:, 6144:6656].rearrange("p (b u j) -> p b u j", b=2, u=8)
        WT = work[:, 6656:7168].rearrange("p (b t) -> p b t", b=2)
        idT = work[:, 7168:7936].rearrange("p (a t) -> p a t", a=3)
        qpT = work[:, 7936:9984].rearrange("p (h t) -> p h t", h=PH)
        skT = work[:, 9984:11008].rearrange("p (h k) -> p h k", h=PH)
        sk = work[:, 11008:12032].rearrange("p (h c) -> p h c", h=PH)
        dec = work[:, 7936:9984]
        cand = work[:, 12032:12288]
        subx = work[:, 12288:12416]
        candx = work[:, 12416:12672]
        sv = work[:, 12672:12928].rearrange("p (h s k) -> p h s k", h=PH, s=2)
        si = work[:, 12928:13184].bitcast(u32).rearrange("p (h s k) -> p h s k", h=PH, s=2)
        sif = work[:, 13184:13440].rearrange("p (h s k) -> p h s k", h=PH, s=2)
        tv = work[:, 13440:13696].rearrange("p (t h k) -> p t h k", t=T, h=PH)
        ids = work[:, 13696:14208].rearrange("p (a t n) -> p a t n", a=2, t=T)
        gate = work[:, 14208:14464].rearrange("p (t h k) -> p t h k", t=T, h=PH)
        tpos = work[:, 14464:14592].bitcast(u32)
        posa = work[:, 14592:14720].bitcast(u32)
        posb = work[:, 14720:14848].bitcast(u32)
        gsum = work[:, 14848:14864]
        A4 = [big[:, ((2 + q) % 3) * 8192:((2 + q) % 3 + 1) * 8192] for q in range(NQ)]
        UT = const[:, 256:2304].rearrange("p (b k i) -> p b k i", b=2, k=KD)
        gain2, bias2 = uring[:, 0:1024], uring[:, 1024:2048]

        P = [ctx.enter_context(nc.psum_tensor(f"P{i}", [128, 512], f32)) for i in range(8)]
        TR, ACTP, GP, Y = P[0:2], P[2], P[3], P[4:8]

        in_table, in_x, in_rows, in_pos = sem("in_table"), sem("in_x"), sem("in_rows"), sem("in_pos")
        in_bcast, in_wf, in_sk, in_ln2 = sem("in_bcast"), sem("in_wf"), sem("in_sk"), sem("in_ln2")
        in_chunk = [sem(f"in_chunk{s}") for s in range(NSLOT)]
        in_u = [sem(f"in_u{s}") for s in range(2)]
        in_v = [sem(f"in_v{s}") for s in range(2)]
        stored = sem("stored")
        pe_rows, cols_ok, csil_ok, csilB_ok = sem("pe_rows"), sem("cols_ok"), sem("csil_ok"), sem("csilB_ok")
        pe_mod, mod_ok = sem("pe_mod"), sem("mod_ok")
        hn_ok, pe_hT, hT_act, hT_dve = sem("hn_ok"), sem("pe_hT"), sem("hT_act"), sem("hT_dve")
        pe_fT, fT_ok, pe_proj, proj_ok = sem("pe_fT"), sem("fT_ok"), sem("pe_proj"), sem("proj_ok")
        pe_gate, gate1_ok, gate2_ok = sem("pe_gate"), sem("gate1_ok"), sem("gate2_ok")
        wf_zero = sem("wf_zero")
        pe_wcs, wcs_ok, pe_fw, fw_ok, pe_mixa = sem("pe_wcs"), sem("wcs_ok"), sem("pe_fw"), sem("fw_ok"), sem("pe_mixa")
        ang_ok, sin_ok, rope_ok, pe_qkT, qkT_ok = sem("ang_ok"), sem("sin_ok"), sem("rope_ok"), sem("pe_qkT"), sem("qkT_ok")
        pe_score, smax_ok, exp_ok, norm_ok = sem("pe_score"), sem("smax_ok"), sem("exp_ok"), sem("norm_ok")
        pe_pT, pT_ok, pe_av, mix_ok = sem("pe_pT"), sem("pT_ok"), sem("pe_av"), sem("mix_ok")
        pe_z = sem("pe_z")
        pe_skT, skT_ok, pe_qp, qp_ok, pe_sub, sub_ok = (sem("pe_skT"), sem("skT_ok"), sem("pe_qp"),
                                                        sem("qp_ok"), sem("pe_sub"), sem("sub_ok"))
        topk_ok, gdiff_ok, gexp_ok, route_ok, pe_idT, idT_ok = (sem("topk_ok"), sem("gdiff_ok"), sem("gexp_ok"),
                                                               sem("route_ok"), sem("pe_idT"), sem("idT_ok"))
        pe_tr0, pe_tr1, ut_act, ut_dve = sem("pe_tr0"), sem("pe_tr1"), sem("ut_act"), sem("ut_dve")
        pe_act, gelu_ok = sem("pe_act"), sem("gelu_ok")
        onehot_ok, pe_g, gmul_ok = sem("onehot_ok"), sem("pe_g"), sem("gmul_ok")
        wt_ok, pe_v = sem("wt_ok"), sem("pe_v")
        sqrt_ok, var_ok = sem("sqrt_ok"), sem("var_ok")
        dve_chain, act_chain = sem("dve_chain"), sem("act_chain")
        fin_ok = sem("fin_ok")

        block = ctx.enter_context(nc.Block())

        def when(eng, s, value):
            if not isinstance(value, int) or value > 0:
                eng.wait_ge(s, value)

        def chunk_in(eng, n):
            eng.wait_ge(in_chunk[n % NSLOT], 16 * (n // NSLOT + 1))

        @block.sync
        def _(sp):
            sp.dma_start(rows[0:48, :], b_ada[0].rearrange("(a n) -> a n", n=128)).then_inc(in_rows, 16)
            sp.dma_start(rows[48:56, :], c[0].rearrange("(a n) -> a n", n=128)).then_inc(in_rows, 16)
            sp.dma_start(rows[56:58, :], b_in[0, 0:FW].rearrange("(a n) -> a n", n=128)).then_inc(in_rows, 16)
            sp.dma_start(const[:, :], table).then_inc(in_table, 16)
            sp.dma_start(x3, x_v).then_inc(in_x, 16)
            sp.dma_start(pos_i[:, :], pos_v, allow_slow_non_contiguous=True).then_inc(in_pos, 16)
            chunk_read = [(pe_mod, 1), (pe_mod, 2), (pe_proj, 4), (pe_proj, 8), (pe_proj, 10), (pe_gate, 2),
                          (pe_mod, 3), (pe_mod, 4)]
            for n, src in enumerate(CHUNKS):
                if n >= NSLOT:
                    sp.wait_ge(*chunk_read[n - NSLOT])
                dst = wc3 if n == WC else slot3[n % NSLOT]
                sp.dma_start(dst, src).then_inc(in_chunk[n % NSLOT], 16)
            def load_u(n, slot):
                sp.dma_start(uring[:, slot * 2048:(slot + 1) * 2048], u_v[:, ds(n * 2048, 2048)])\
                  .then_inc(in_u[slot], 16)

            def load_v(n, slot):
                sp.dma_start(vring[:, slot * 2048:(slot + 1) * 2048], v_v[:, ds(n * 2048, 2048)])\
                  .then_inc(in_v[slot], 16)

            sp.wait_ge(pe_mixa, 2)
            sp.wait_ge(gate2_ok, 2)
            for n in range(2):
                load_u(n, n)
            with sp.Fori(0, 15) as i:
                for b in range(2):
                    sp.wait_ge(pe_tr1, 4 * i + 2 * b + 2)
                    load_u(2 * i + 2 + b, b)
            sp.wait_ge(topk_ok, 1)
            for n in range(2):
                load_v(n, n)
            def next_u(n, slot, i):
                sp.wait_ge(pe_tr1, 4 * i + 2 * slot + 62)
                load_u(n, slot)

            def next_v(n, slot, i):
                sp.wait_ge(pe_v, 4 * i + 2 * slot - 2)
                load_v(n, slot)

            for b in range(2):
                next_u(32 + b, b, 0)
            with sp.Fori(1, 16) as i:
                for b in range(2):
                    next_u(2 * i + 32 + b, b, i)
                    next_v(2 * i + b, b, i)
            with sp.Fori(16, 32) as i:
                for b in range(2):
                    next_v(2 * i + b, b, i)
            sp.wait_ge(stored, 32)

        @block.gpsimd
        def _(pool):
            pool.memset(wfd, 0.0).then_inc(wf_zero, 1)
            pool.wait_ge(wf_zero, 1)
            for g in range(4):
                h0 = (g % 2) * 64
                pool.dma_start(wfd[h0:h0 + 64, g // 2, h0:h0 + 64], w_fourier[0, g]).then_inc(in_wf, 16)
            def gated(q, jj, b, j):
                pool.wait_ge(gmul_ok, 32 * (q + 1))
                when(pool, pe_v, j - 1)
                pool.tensor_copy(WT[:, b, :], A4[q][:, ds(jj * S, S)]).then_inc(wt_ok, 1)

            for q in range(NQ):
                first = 0
                if q == 0:
                    for b in range(4):
                        gated(0, b, b % 2, b)
                    first = 1
                with pool.Fori(first, QJ // BODY) as i:
                    for b in range(BODY):
                        gated(q, i * BODY + b, b % 2, i * BODY + b + QJ * q)

        @block.scalar
        def _(act):
            n_chain = [0]

            def link(ins):
                n_chain[0] += 1
                ins.then_inc(act_chain, 1)
                act.wait_ge(act_chain, n_chain[0])

            for dst, src in ((bin_row, b_in[0, FW:]), (bout_row, b_out[0]), (gain1, ln1_gain[0]),
                             (bias1, ln1_bias[0]), (g1s[:, :], b_ada[0, 2 * D:3 * D]),
                             (g2s[:, :], b_ada[0, 5 * D:6 * D])):
                act.dma_start(dst, src.partition_broadcast(128)).then_inc(in_bcast, 16)
            act.wait_ge(cols_ok, 1)
            act.activation(csil[:, :], cols[:, 48:56], ACT.Silu).then_inc(csil_ok, 1)

            def root(n):
                act.wait_ge(var_ok, n)
                act.activation(stat[:, 14:15], stat[:, 13:14], ACT.Sqrt).then_inc(sqrt_ok, 1)

            root(1)
            root(2)
            def hT_out(m, turn):
                act.wait_ge(mod_ok, 2 * turn)
                for k in range(4):
                    act.wait_ge(pe_hT, 4 * (turn - 1) + k // 2 + 1)
                    act.activation(hT[:, k, :], P[2 + k // 2][:, (k % 2) * S:(k % 2 + 1) * S], ACT.Identity,
                                   bias=modc[:, m + k:m + k + 1], scale=modc[:, m + 8 + k:m + 9 + k])\
                       .then_inc(hT_act, 1)

            hT_out(0, 1)
            for n in range(2):
                act.wait_ge(pe_fT, n + 1)
                act.activation(fT[:, n, :], P[6 + n][:, 0:S], ACT.Identity, bias=cols[:, 56 + n:57 + n])\
                   .then_inc(fT_ok, 1)
            act.wait_ge(ang_ok, 1)
            act.activation(rope_cs, rope_w, ACT.Sin).then_inc(sin_ok, 1)
            for n in range(2):
                act.wait_ge(pe_wcs, n + 1)
                act.activation(wcs[:, n, :, :], P[6 + n][:, 0:256].rearrange("p (c m) -> p c m", c=2), ACT.Copy)\
                   .then_inc(wcs_ok, 1)
            for s in range(2):
                act.wait_ge(pe_fw, s + 1)
                act.activation(fw[:, s, :, :, :], P[6 + s][:, :].rearrange("p (n c m) -> p n c m", n=2, c=2),
                               ACT.Copy).then_inc(fw_ok, 1)
            for n in range(2):
                act.wait_ge(pe_mixa, n + 1)
                act.activation(mixT[:, n, :], P[6 + n][:, 0:S], ACT.Copy).then_inc(mix_ok, 1)
            for h in range(NH + 1):
                if h < NH:
                    act.wait_ge(smax_ok, h + 1)
                    for q in range(2):
                        act.activation(prob[:, h % 2, q, :], prob[:, h % 2, q, :], ACT.Exp,
                                       bias=rmax[:, 4 * (h % 2) + 2 + q:4 * (h % 2) + 3 + q],
                                       accum_out=rsum[:, 4 * (h % 2) + q:4 * (h % 2) + q + 1]).then_inc(exp_ok, 1)
                if h >= 1:
                    g = h - 1
                    act.wait_ge(pe_pT, g + 1)
                    if g >= 2:
                        act.wait_ge(pe_av, g - 1)
                    act.activation(probT[:, g % 2, :, :], P[2 + g % 2][:, :].rearrange("p (k q) -> p k q", k=2),
                                   ACT.Copy).then_inc(pT_ok, 1)
                    if g % 2:
                        act.wait_ge(pe_av, g + 1)
                        act.activation(mixT[:, 2 + g // 2, :], P[4 + (g // 2) % 2][:, 0:S], ACT.Copy)\
                           .then_inc(mix_ok, 1)
            act.wait_ge(pe_av, NH)
            act.dma_start(sk, peer_subkeys[0].rearrange("h s k c -> k h s c")).then_inc(in_sk, 16)
            for n in range(2):
                act.wait_ge(pe_skT, n + 1)
                act.activation(skT[:, 4 * n:4 * n + 4, :], P[4 + n][:, :].rearrange("p (h k) -> p h k", h=4),
                               ACT.Copy).then_inc(skT_ok, 1)
            for n in range(3, 7):
                root(n)
            hT_out(16, 2)
            for n in range(4):
                act.wait_ge(pe_qp, n + 1)
                act.activation(qpT[:, 2 * n:2 * n + 2, :], P[(6, 7, 0, 1)[n]][:, :].rearrange("p (h t) -> p h t", h=2),
                               ACT.Copy).then_inc(qp_ok, 1)
            for n in range(8):
                t, s, hh = n // 4, n // 2 % 2, n % 2
                act.wait_ge(pe_sub, n + 1)
                act.activation(sub[:, t, s, 4 * hh:4 * hh + 4, :],
                               P[(2, 3, 4, 5, 6, 7, 0, 1)[n]][:, :].rearrange("p (h k) -> p h k", h=4), ACT.Copy)\
                   .then_inc(sub_ok, 1)

            def ut_out(b, j):
                act.wait_ge(pe_tr0, j + 1)
                when(act, pe_act, j - 1)
                act.activation(UT[:, b, 0:4, :], TR[0][:, :].rearrange("p (k i) -> p k i", k=4), ACT.Copy)\
                   .then_inc(ut_act, 1)

            def gelu(q, jj, j):
                act.wait_ge(pe_act, j + 1)
                if q == 3:
                    act.wait_ge(wt_ok, QJ)
                act.activation(A4[q][:, ds(jj * S, S)], ACTP[:, 0:S], ACT.Gelu).then_inc(gelu_ok, 1)

            act.wait_ge(gate2_ok, 2)
            ut_out(0, 0)
            for q in range(NQ):
                last = q == NQ - 1
                if q == 0:
                    for jj in range(BODY):
                        ut_out((jj + 1) % 2, jj + 1)
                        gelu(0, jj, jj)
                with act.Fori(int(q == 0), QJ // BODY - last) as i:
                    for b in range(BODY):
                        ut_out((b + 1) % 2, i * BODY + b + 1 + QJ * q)
                        gelu(q, i * BODY + b, i * BODY + b + QJ * q)
                if last:
                    for jj in range(QJ - BODY, QJ):
                        if jj < QJ - 1:
                            ut_out((jj + 1) % 2, jj + 1 + QJ * q)
                        gelu(q, jj, jj + QJ * q)
                if q == 0:
                    act.wait_ge(gdiff_ok, 1)
                    act.activation(gate, gate, ACT.Exp).then_inc(gexp_ok, 1)
            act.wait_ge(pe_tr1, 4 * QJ)
            for dst, src in ((gain2, ln2_gain[0]), (bias2, ln2_bias[0])):
                act.dma_start(dst, src.partition_broadcast(128)).then_inc(in_ln2, 16)
            for t in range(T):
                root(7 + t)
                act.wait_ge(fin_ok, t + 1)
                act.dma_start(out_v[:, t, :], x3[:, t, :]).then_inc(stored, 16)
            act.wait_ge(stored, 32)

        @block.vector
        def _(dve):
            count = {}

            def link(ins, signal=None):
                s = dve_chain if signal is None else signal
                count[id(s)] = count.get(id(s), 0) + 1
                ins.then_inc(s, 1)
                dve.wait_ge(s, count[id(s)])

            roots = [0]

            def normalise(dst, src):
                for n in range(2):
                    last = dve.bn_stats(stat[:, 6 * n:6 * n + 6], src[:, 512 * n:512 * n + 512])
                    link(last)
                link(dve.bn_aggr(stat[:, 12:14], stat[:, 0:12].rearrange("p (a b) -> p a b", a=2)))
                roots[0] += 1
                link(dve.tensor_scalar(stat[:, 13:14], stat[:, 13:14], EPS, None, ALU.add), var_ok)
                dve.wait_ge(sqrt_ok, roots[0])
                link(dve.reciprocal(stat[:, 15:16], stat[:, 14:15]))
                return dve.tensor_scalar(dst, src, stat[:, 12:13], stat[:, 15:16], ALU.subtract, ALU.mult)

            def transposed_h(m, turn):
                for k in range(4, 8):
                    dve.wait_ge(pe_hT, 4 * (turn - 1) + k // 2 + 1)
                    dve.tensor_scalar(hT[:, k, :], P[2 + k // 2][:, (k % 2) * S:(k % 2 + 1) * S],
                                      modc[:, m + 8 + k:m + 9 + k], modc[:, m + k:m + k + 1],
                                      ALU.mult, ALU.add).then_inc(hT_dve, 1)

            def modulation(chunk, m, one, n):
                dve.wait_ge(pe_mod, n)
                link(dve.scalar_tensor_tensor(modc[:, m:m + 8], P[1 - m // 8 % 2][:, m:m + 8], one,
                                              cols[:, 8 * chunk:8 * chunk + 8], ALU.add, ALU.add), mod_ok)

            dve.wait_ge(pe_rows, 1)
            link(dve.tensor_copy(cols[:, :], P[0][:, 0:58]), cols_ok)
            dve.wait_ge(csil_ok, 1)
            dve.tensor_copy(csilB, csil[:, :].unsqueeze(2).to_broadcast([128, 8, 128])).then_inc(csilB_ok, 1)
            dve.wait_ge(in_x, 16)
            for t in range(T):
                link(normalise(hn[:, t, :], x3[:, t, :]), hn_ok)
            dve.wait_ge(in_pos, 16)
            dve.wait_ge(in_table, 16)
            link(dve.tensor_copy(pos_f[:, :], pos_i[:, :]))
            for t in range(T):
                for a in range(2):
                    link(dve.tensor_scalar(rope_w[:, a, t, :], invf, pos_f[:, t:t + 1], None, ALU.mult))
            TURN = 2.0 * math.pi
            C1 = 6.28125
            C2 = float(np.float32(np.round((TURN - C1) * 2 ** 21) / 2 ** 21))
            C3 = float(np.float32(TURN - C1 - C2))
            ROUND = 12582912.0
            for a, lead in ((0, 0.25), (1, 0.0)):
                w, n = rope_w[:, a, :, :], rope_cs[:, a, :, :]
                link(dve.tensor_scalar(n, w, 1.0 / TURN, lead, ALU.mult, ALU.add))
                link(dve.tensor_scalar(n, n, ROUND, None, ALU.add))
                link(dve.tensor_scalar(n, n, ROUND, None, ALU.subtract))
                for part in (C1, C2, C3):
                    link(dve.scalar_tensor_tensor(w, n, -part, w, ALU.mult, ALU.add))
                if a == 0:
                    link(dve.tensor_scalar(w, w, math.pi / 2, None, ALU.add))
                lim = 3.1415925
                link(dve.tensor_scalar(w, w, -lim, lim, ALU.max, ALU.min))
            link(dve.tensor_copy(pos_f[:, :], pos_i[:, :]), ang_ok)
            modulation(0, 0, 0.0, 1)
            modulation(1, 8, 1.0, 2)
            transposed_h(0, 1)
            dve.wait_ge(in_bcast, 16 * 6)
            dve.wait_ge(hT_dve, 4)
            dve.wait_ge(pe_hT, 4)
            for g, (t, c0, n) in enumerate(GROUPS):
                dve.wait_ge(pe_proj, g + 1)
                dve.tensor_tensor(qkv[:, t, c0:c0 + n], P[2 + g % 4][:, 0:n], bin_row[:, c0:c0 + n], ALU.add)\
                   .then_inc(proj_ok, 1)
            for n in range(2):
                dve.wait_ge(pe_gate, n + 1)
                dve.scalar_tensor_tensor(g1s[:, 512 * n:512 * n + 512], P[6 + n][:, :], 1.0,
                                         g1s[:, 512 * n:512 * n + 512], ALU.add, ALU.add).then_inc(gate1_ok, 1)
            dve.wait_ge(proj_ok, len(GROUPS))
            dve.wait_ge(sin_ok, 1)
            for t in range(T):
                qk = qkv[:, t, 0:2 * AW].rearrange("p (n two f) -> p n two f", two=2, f=32)
                cs = rope_cs[:, 0, t, :].unsqueeze(1).to_broadcast([128, 24, 32])
                sn = rope_cs[:, 1, t, :].unsqueeze(1).to_broadcast([128, 24, 32])
                t1, t2 = qk[:, :, 0, :], qk[:, :, 1, :]
                link(dve.tensor_tensor(rtmp[:, 0], t1, sn, ALU.mult))
                link(dve.tensor_tensor(rtmp[:, 1], t2, sn, ALU.mult))
                link(dve.tensor_tensor(t1, t1, cs, ALU.mult))
                link(dve.tensor_tensor(t2, t2, cs, ALU.mult))
                link(dve.tensor_tensor(t1, t1, rtmp[:, 1], ALU.subtract))
                link(dve.tensor_tensor(t2, t2, rtmp[:, 0], ALU.add), rope_ok)
            for b in range(6):
                dve.wait_ge(pe_qkT, b + 1)
                dve.tensor_copy(qkT[:, 2 * b:2 * b + 2, :], P[2 + b % 4][:, :].rearrange("p (n t) -> p n t", n=2))\
                   .then_inc(qkT_ok, 1)
            modulation(3, 16, 0.0, 3)
            modulation(4, 24, 1.0, 4)
            def score_max(h):
                dve.wait_ge(pe_score, h + 1)
                if h >= 2:
                    dve.wait_ge(pe_pT, h - 1)
                r = rmax[:, 4 * (h % 2):4 * (h % 2) + 4]
                for q in range(2):
                    link(dve.tensor_tensor_reduce(out=prob[:, h % 2, q, :], in0=P[h % 2][:, q * S:(q + 1) * S],
                                                  in1=bias_c[:, q, :], scale=HD ** -0.5, scalar=-3.0e38,
                                                  op0=ALU.add, op1=ALU.max, accum_out=r[:, q:q + 1]))
                link(dve.tensor_scalar(r[:, 2:4], r[:, 0:2], -1.0, None, ALU.mult), smax_ok)

            def over_sum(h):
                dve.wait_ge(exp_ok, 2 * h + 2)
                r = rsum[:, 4 * (h % 2):4 * (h % 2) + 4]
                link(dve.reciprocal(r[:, 2:4], r[:, 0:2]))
                for q in range(2):
                    dve.tensor_scalar(prob[:, h % 2, q, :], prob[:, h % 2, q, :], r[:, 2 + q:3 + q], None,
                                      ALU.mult).then_inc(norm_ok, 1)

            score_max(0)
            for h in range(NH):
                if h + 1 < NH:
                    score_max(h + 1)
                over_sum(h)
            for t in range(T):
                for n in range(2):
                    s = slice(512 * n, 512 * n + 512)
                    dve.wait_ge(pe_z, 2 * t + n + 1)
                    link(dve.tensor_tensor(hn[:, t, s], P[(6, 7, 0, 1)[2 * t + n]][:, :], bout_row[:, s], ALU.add))
                link(dve.tensor_tensor(hn[:, t, :], hn[:, t, :], g1s[:, :], ALU.mult))
                link(dve.scalar_tensor_tensor(x3[:, t, :], x3[:, t, :], ALPHA, hn[:, t, :], ALU.mult, ALU.add))
                link(normalise(x3[:, t, :], x3[:, t, :]))
                link(dve.tensor_tensor(x3[:, t, :], x3[:, t, :], gain1, ALU.mult))
                link(dve.tensor_tensor(x3[:, t, :], x3[:, t, :], bias1, ALU.add))
                link(normalise(hn[:, t, :], x3[:, t, :]), hn_ok)
            transposed_h(16, 2)
            for n in range(2):
                dve.wait_ge(pe_gate, n + 3)
                dve.scalar_tensor_tensor(g2s[:, 512 * n:512 * n + 512], P[2 + n][:, :], 1.0,
                                         g2s[:, 512 * n:512 * n + 512], ALU.add, ALU.add).then_inc(gate2_ok, 1)

            def ut_out(b, j):
                dve.wait_ge(pe_tr1, j + 1)
                when(dve, pe_act, j - 1)
                dve.tensor_copy(UT[:, b, 4:8, :], TR[1][:, :].rearrange("p (k i) -> p k i", k=4))\
                   .then_inc(ut_dve, 1)

            def top16(values, scratch, best, where):
                link(dve.max(best[:, 0:8], values))
                link(dve.max_index(where[:, 0:8], best[:, 0:8], values))
                link(dve.match_replace(scratch, best[:, 0:8], values, -3.0e38))
                link(dve.max(best[:, 8:16], scratch))
                link(dve.max_index(where[:, 8:16], best[:, 8:16], scratch))

            def head_keys(t, h):
                for s in range(2):
                    top16(sub[:, t, s, h, :], subx, sv[:, h, s, :], si[:, h, s, :])

            def head_pairs(t, h):
                c3 = cand.rearrange("p (a b) -> p a b", a=TOPK)
                link(dve.tensor_tensor(c3, sv[:, h, 0, :].unsqueeze(2).to_broadcast([128, TOPK, TOPK]),
                                       sv[:, h, 1, :].unsqueeze(1).to_broadcast([128, TOPK, TOPK]), ALU.add))
                top16(cand, candx, tv[:, t, h, :], tpos[:, h * TOPK:(h + 1) * TOPK])

            def key_ids(t):
                link(dve.tensor_copy(sif, si))
                link(dve.tensor_scalar(posa, tpos, 4, None, ALU.logical_shift_right))
                link(dve.tensor_scalar(posb, tpos, 15, None, ALU.bitwise_and))
                i16 = iota[:, 0:16].unsqueeze(1).to_broadcast([128, 128, 16])
                d3 = dec.rearrange("p (n a) -> p n a", a=16)
                d4 = dec.rearrange("p (h k a) -> p h k a", h=PH, k=TOPK)
                for s, where in ((0, posa), (1, posb)):
                    link(dve.tensor_tensor(d3, where.unsqueeze(2).to_broadcast([128, 128, 16]), i16, ALU.is_equal))
                    link(dve.tensor_tensor(d4, d4, sif[:, :, s, :].unsqueeze(2).to_broadcast([128, PH, TOPK, 16]),
                                           ALU.mult))
                    link(dve.tensor_reduce(ids[:, s, t, :], d3, AX.X, ALU.add))

            dve.wait_ge(sub_ok, 8)
            ut_out(0, 0)
            for j in range(QJ):
                ut_out((j + 1) % 2, j + 1)
                t, h = j // 16, j % 16 // 2
                if j % 2 == 0:
                    head_keys(t, h)
                else:
                    head_pairs(t, h)
                if j % 16 == 15:
                    key_ids(t)
            link(dve.tensor_tensor(gate, tv, tv[:, :, :, 0:1].to_broadcast([128, T, PH, TOPK]), ALU.subtract), topk_ok)
            link(dve.memset(gsum, 0.0), gdiff_ok)
            dve.wait_ge(gexp_ok, 1)
            g2 = gsum.rearrange("p (t h) -> p t h", t=T)
            link(dve.tensor_reduce(g2, gate, AX.X, ALU.add))
            link(dve.reciprocal(gsum, gsum))
            link(dve.tensor_tensor(gate, gate, g2.unsqueeze(3).to_broadcast([128, T, PH, TOPK]), ALU.mult), route_ok)
            for t in range(T):
                dve.wait_ge(pe_idT, t + 1)
                link(dve.tensor_copy(idT[:, :, 128 * t:128 * t + 128],
                                     GP[:, 0:384].rearrange("p (a t) -> p a t", a=3)), idT_ok)

            def onehots(q, g, b):
                for u in range(8):
                    tok = g * 8 + u
                    dve.tensor_scalar(OI[:, b, u, :], iota, idT[:, 0, ds(tok, 1)], None, ALU.is_equal)
                    last = dve.tensor_scalar(OJ[:, b, u, :], iota[:, QJ * q:QJ * q + QJ], idT[:, 1, ds(tok, 1)],
                                             idT[:, 2, ds(tok, 1)], ALU.is_equal, ALU.mult)
                last.then_inc(onehot_ok, 1)

            def apply_gates(q, g, n):
                dve.wait_ge(pe_g, n + 1)
                dve.wait_ge(gelu_ok, QJ * (q + 1))
                a = A4[q].rearrange("p (j t) -> p j t", t=S)[:, :, ds(g * 8, 8)]
                dve.tensor_tensor(a, a, GP[:, 0:256].rearrange("p (u j) -> p j u", u=8), ALU.mult)\
                   .then_inc(gmul_ok, 1)

            for q in range(1, NQ):
                last = q == NQ - 1
                with dve.Fori(0, QJ // BODY - last) as i:
                    for b in range(BODY):
                        ut_out((b + 1) % 2, i * BODY + b + 1 + QJ * q)
                        onehots(q - 1, i * BODY + b, b % 2)
                        apply_gates(q - 1, i * BODY + b, i * BODY + b + QJ * (q - 1))
                if last:
                    for jj in range(QJ - BODY, QJ):
                        if jj < QJ - 1:
                            ut_out((jj + 1) % 2, jj + 1 + QJ * q)
                        onehots(q - 1, jj, jj % 2)
                        apply_gates(q - 1, jj, jj + QJ * (q - 1))
            with dve.Fori(0, QJ // 2) as i:
                for b in range(2):
                    onehots(NQ - 1, i * 2 + b, b)
                    apply_gates(NQ - 1, i * 2 + b, i * 2 + b + QJ * (NQ - 1))
            dve.wait_ge(in_ln2, 32)
            dve.wait_ge(pe_v, 4 * QJ)
            for t in range(T):
                ys = big[:, 1024 * t:1024 * t + 1024]
                for n in range(2):
                    s = slice(512 * n, 512 * n + 512)
                    link(dve.tensor_tensor(ys[:, s], Y[2 * t + n][:, :], g2s[:, s], ALU.mult))
                link(dve.scalar_tensor_tensor(x3[:, t, :], x3[:, t, :], ALPHA, ys, ALU.mult, ALU.add))
                link(normalise(x3[:, t, :], x3[:, t, :]))
                link(dve.tensor_tensor(x3[:, t, :], x3[:, t, :], gain2, ALU.mult))
                link(dve.tensor_tensor(x3[:, t, :], x3[:, t, :], bias2, ALU.add), fin_ok)

        @block.tensor
        def _(pe):
            mm = pe.matmul

            def transpose(dst, src):
                return pe.transpose(dst, src, ident[0:src.shape[0], 0:src.shape[0]])

            def mod_columns(n, m):
                chunk_in(pe, n)
                for a in range(8):
                    for k in range(KD):
                        last = mm(P[1 - m // 8 % 2][:, m + a:m + a + 1], slot3[n % NSLOT][:, k, a * 128:a * 128 + 128],
                                  csil[:, k:k + 1], start=(k == 0), stop=(k == KD - 1))
                last.then_inc(pe_mod, 1)

            def gate_rows(n, banks):
                chunk_in(pe, n)
                for a in range(2):
                    for k in range(KD):
                        last = mm(banks[a][:, :], csilB[:, k, :], slot3[n % NSLOT][:, k, 512 * a:512 * a + 512],
                                  start=(k == 0), stop=(k == KD - 1))
                    last.then_inc(pe_gate, 1)

            def h_transposes(turn):
                pe.wait_ge(hn_ok, 2 * turn)
                for b in range(4):
                    for kk in range(2):
                        for t in range(T):
                            k = 2 * b + kk
                            last = transpose(P[2 + b][:, kk * S + t * 128:kk * S + t * 128 + 128],
                                             hn[:, t, k * 128:k * 128 + 128])
                    last.then_inc(pe_hT, 1)

            pe.wait_ge(in_table, 16)
            pe.wait_ge(in_rows, 48)
            transpose(P[0][:, 0:58], rows).then_inc(pe_rows, 1)
            pe.wait_ge(csil_ok, 1)
            mod_columns(SH1, 0)
            mod_columns(SC1, 8)
            h_transposes(1)
            pe.wait_ge(hT_act, 4)
            pe.wait_ge(hT_dve, 4)
            chunk_in(pe, WA)
            for n in range(2):
                for k in range(KD):
                    last = mm(P[6 + n][:, 0:S], slot3[WA % NSLOT][:, k, n * 128:n * 128 + 128], hT[:, k, :],
                              start=(k == 0), stop=(k == KD - 1))
                last.then_inc(pe_fT, 1)
            for g, (t, c0, n) in enumerate(GROUPS):
                w, col, n_chunk = ((slot3[WA % NSLOT], c0 + FW, WA) if c0 < 768 else
                                   (slot3[WB % NSLOT], c0 - 768, WB) if c0 < 1792 else (wc3, c0 - 1792, WC))
                chunk_in(pe, n_chunk)
                if g >= 4:
                    pe.wait_ge(proj_ok, g - 3)
                for k in range(KD):
                    last = mm(P[2 + g % 4][:, 0:n], hT[:, k, t * 128:t * 128 + 128], w[:, k, col:col + n],
                              start=(k == 0), stop=(k == KD - 1))
                last.then_inc(pe_proj, 1)
            pe.wait_ge(csilB_ok, 1)
            pe.wait_ge(fT_ok, 2)
            gate_rows(GT1, (P[6], P[7]))
            pe.wait_ge(mod_ok, 2)
            pe.wait_ge(gate1_ok, 2)
            mod_columns(SH2, 16)
            mod_columns(SC2, 24)
            pe.wait_ge(in_wf, 64)
            for n in range(2):
                for cs in range(2):
                    last = mm(P[6 + n][:, cs * 128:cs * 128 + 128], chan_c[:, cs, :], wfd[:, n, :], start=True, stop=True)
                last.then_inc(pe_wcs, 1)
            pe.wait_ge(wcs_ok, 2)
            for s in range(2):
                for n in range(2):
                    last = mm(P[6 + s][:, n * 256:n * 256 + 256], fT[:, n, s * 128:s * 128 + 128],
                              wcs[:, n, :, :].rearrange("p c m -> p (c m)"), start=True, stop=True)
                last.then_inc(pe_fw, 1)
            pe.wait_ge(fw_ok, 2)
            for n in range(2):
                for i, (cs, s) in enumerate(((0, 0), (0, 1), (1, 0), (1, 1))):
                    last = mm(P[6 + n][:, 0:S], fw[:, s, n, cs, :], seq_c[:, cs, s, :], start=(i == 0), stop=(i == 3))
                last.then_inc(pe_mixa, 1)
            pe.wait_ge(rope_ok, 2)
            for b in range(6):
                if b >= 4:
                    pe.wait_ge(qkT_ok, b - 3)
                for kk in range(2):
                    for t in range(T):
                        n = 2 * b + kk
                        last = transpose(P[2 + b % 4][:, kk * S + t * 128:kk * S + t * 128 + 128],
                                         qkv[:, t, n * 128:n * 128 + 128])
                last.then_inc(pe_qkT, 1)

            def scores(h):
                p0 = (h % 2) * 64
                if h >= 2:
                    pe.wait_ge(smax_ok, h - 1)
                for q in range(2):
                    last = mm(P[h % 2][:, q * S:(q + 1) * S], qkT[p0:p0 + 64, h // 2, q * 128:q * 128 + 128],
                              qkT[p0:p0 + 64, 6 + h // 2, :], start=True, stop=True)
                last.then_inc(pe_score, 1)

            def attend(h):
                pe.wait_ge(norm_ok, 2 * h + 2)
                if h >= 2:
                    pe.wait_ge(pT_ok, h - 1)
                for k in range(2):
                    for q in range(2):
                        last = transpose(P[2 + h % 2][:, k * S + q * 128:k * S + q * 128 + 128],
                                         prob[:, h % 2, q, k * 128:k * 128 + 128])
                last.then_inc(pe_pT, 1)

            def values(h):
                p0 = (h % 2) * 64
                pe.wait_ge(pT_ok, h + 1)
                if h >= 4:
                    pe.wait_ge(mix_ok, 2 + h // 2 - 1)
                for k in range(2):
                    last = mm(P[4 + (h // 2) % 2][p0:p0 + 64, 0:S], qkv[:, k, 2 * AW + h * HD:2 * AW + h * HD + HD],
                              probT[:, h % 2, k, :], start=(k == 0), stop=(k == 1))
                last.then_inc(pe_av, 1)

            pe.wait_ge(qkT_ok, 6)
            pe.wait_ge(mod_ok, 4)
            scores(0)
            scores(1)
            for h in range(NH):
                attend(h)
                if h + 2 < NH:
                    scores(h + 2)
                values(h)
            pe.wait_ge(mix_ok, 8)
            pe.wait_ge(smax_ok, NH)
            chunk_in(pe, WO)
            for t in range(T):
                for n in range(2):
                    for k in range(KD):
                        last = mm(P[(6, 7, 0, 1)[2 * t + n]][:, :], mixT[:, k, t * 128:t * 128 + 128],
                                  slot3[WO % NSLOT][:, k, 512 * n:512 * n + 512], start=(k == 0), stop=(k == KD - 1))
                    last.then_inc(pe_z, 1)
            pe.wait_ge(in_sk, 16)
            for n in range(2):
                for h in range(4):
                    last = transpose(P[4 + n][:, h * 128:h * 128 + 128], sk[:, 4 * n + h, :])
                last.then_inc(pe_skT, 1)
            pe.wait_ge(skT_ok, 2)
            h_transposes(2)
            pe.wait_ge(hT_act, 8)
            pe.wait_ge(hT_dve, 8)
            chunk_in(pe, WPQ)
            for n in range(4):
                for hh in range(2):
                    h = 2 * n + hh
                    for k in range(KD):
                        last = mm(P[(6, 7, 0, 1)[n]][:, hh * S:hh * S + S],
                                  slot3[WPQ % NSLOT][:, k, h * 128:h * 128 + 128], hT[:, k, :],
                                  start=(k == 0), stop=(k == KD - 1))
                last.then_inc(pe_qp, 1)
            pe.wait_ge(qp_ok, 4)
            gate_rows(GT2, (P[2], P[3]))
            pe.wait_ge(gate2_ok, 2)
            for n in range(8):
                t, s, hh = n // 4, n // 2 % 2, n % 2
                for h in range(4 * hh, 4 * hh + 4):
                    last = mm(P[(2, 3, 4, 5, 6, 7, 0, 1)[n]][:, (h % 4) * 128:(h % 4) * 128 + 128],
                              qpT[64 * s:64 * s + 64, h, t * 128:t * 128 + 128], skT[64 * s:64 * s + 64, h, :],
                              start=True, stop=True)
                last.then_inc(pe_sub, 1)
            pe.wait_ge(sub_ok, 8)

            def u_transposes(slot, j, turn):
                if slot % 2 == 0:
                    pe.wait_ge(in_u[slot // 2], turn)
                for half, read, done in ((0, ut_act, pe_tr0), (1, ut_dve, pe_tr1)):
                    when(pe, read, j)
                    for k in range(4):
                        kk = 4 * half + k
                        last = transpose(TR[half][:, k * 128:k * 128 + 128],
                                         uring[:, slot * D + kk * 128:slot * D + kk * 128 + 128])
                    last.then_inc(done, 1)

            def u_product(b, j):
                pe.wait_ge(ut_act, j + 1)
                pe.wait_ge(ut_dve, j + 1)
                when(pe, gelu_ok, j)
                for k in range(KD):
                    last = mm(ACTP[:, 0:S], UT[:, b, k, :], hT[:, k, :], start=(k == 0), stop=(k == KD - 1))
                last.then_inc(pe_act, 1)

            def gates(b, n):
                pe.wait_ge(onehot_ok, n + 1)
                when(pe, gmul_ok, n)
                for u in range(8):
                    last = mm(GP[:, u * QJ:u * QJ + QJ], OI[:, b, u, :], OJ[:, b, u, :], start=True, stop=True)
                last.then_inc(pe_g, 1)

            def v_product(slot, j, turn, first=False, final=False):
                if slot % 2 == 0:
                    pe.wait_ge(in_v[slot // 2], turn)
                pe.wait_ge(wt_ok, j + 1)
                for t in range(T):
                    for n in range(2):
                        last = mm(Y[2 * t + n][:, :], WT[:, slot % 2, t * 128:t * 128 + 128],
                                  vring[:, slot * D + 512 * n:slot * D + 512 * n + 512], start=first, stop=final)
                last.then_inc(pe_v, 1)

            u_transposes(0, 0, 16)
            for q in range(NQ + 2):
                u_on, g_on, v_on = q < NQ, 1 <= q < NQ + 1, q >= 2

                def steps(i, b):
                    jj = i * BODY + b
                    if u_on and not (q == NQ - 1 and isinstance(i, int) and jj == QJ - 1):
                        u_transposes((b + 1) % BODY, jj + 1 + QJ * q, 16 * (i + QJ // BODY * q + 1 + (b == BODY - 1)))
                    if u_on:
                        u_product(b % 2, jj + QJ * q)
                    if g_on:
                        gates(b % 2, jj + QJ * (q - 1))
                    if v_on:
                        v_product(b, jj + QJ * (q - 2), 16 * (i + QJ // BODY * (q - 2) + 1),
                                  first=q == 2 and isinstance(i, int) and jj == 0,
                                  final=q == NQ + 1 and isinstance(i, int) and jj == QJ - 1)

                head = q <= 2
                tail = q in (NQ - 1, NQ + 1)
                if q == 1:
                    pe.wait_ge(route_ok, 1)
                    for t in range(T):
                        if t:
                            pe.wait_ge(idT_ok, t)
                        for a in range(3):
                            src = ids[:, a, t, :] if a < 2 else gate[:, t, :, :].rearrange("p h k -> p (h k)")
                            last = transpose(GP[:, a * 128:a * 128 + 128], src)
                        last.then_inc(pe_idT, 1)
                    pe.wait_ge(idT_ok, 2)
                if head:
                    for b in range(BODY):
                        steps(0, b)
                with pe.Fori(1 if head else 0, QJ // BODY - (1 if tail else 0)) as i:
                    for b in range(BODY):
                        steps(i, b)
                if tail:
                    for b in range(BODY):
                        steps(QJ // BODY - 1, b)


GROUPS = [(t, c, 384) for c in (0, 384) for t in range(2)] + \
         [(t, c, 512) for c in (768, 1280) for t in range(2)] + [(t, 1792, 512) for t in range(2)]


def constant_table():
    tab = np.zeros((128, C_END), np.float64)
    p = np.arange(128)
    tab[:, 0:128] = np.eye(128)
    tab[:, C_IOTA:C_IOTA + 128] = np.arange(128)
    q = p[:, None, None] + 128 * np.arange(2)[None, :, None]
    off = np.arange(S)[None, None, :] - q
    n = np.zeros(off.shape)
    for window, dil in ((128, 1), (512, 4), (2048, 16)):
        n += (off % dil == 0) & (np.abs(off) <= window // 2)
    tab[:, C_BIAS:C_SEQ] = (np.where(n > 0, np.log(np.maximum(n, 1)), -1e30) * HD ** 0.5).reshape(128, -1)
    s = p[:, None, None] + 128 * np.arange(2)[None, :, None]
    ang = 2 * np.pi * ((s * np.arange(S)[None, None, :]) % S) / S
    norm = 1.0 / math.sqrt(S * 64)
    tab[:, C_SEQ:C_CHAN] = np.stack([np.cos(ang) * norm, -np.sin(ang) * norm], 1).reshape(128, -1)
    c = np.arange(64)
    ang = 2 * np.pi * (np.outer(c, c) % 64) / 64
    for k, m in enumerate((np.cos(ang), np.sin(ang))):
        for g in range(2):
            tab[64 * g:64 * g + 64, C_CHAN + 128 * k + 64 * g:C_CHAN + 128 * k + 64 * g + 64] = m
    inv = (np.float32(10000.0) ** (-np.arange(32, dtype=np.float32) / np.float32(32))).astype(np.float32)
    tab[:, C_INVF:C_INVF + 32] = inv
    return tab.astype(np.float32)


_INS = ["x", "c", "positions", "w_ada", "b_ada", "w_in", "b_in", "w_fourier", "w_out", "b_out", "ln1_gain",
        "ln1_bias", "w_peer_q", "peer_subkeys", "peer_u", "peer_v", "ln2_gain", "ln2_bias"]


def kernel(**inputs):
    import concourse.bacc as bacc
    from concourse.bass_utils import run_bass_kernel_spmd

    nc = bacc.Bacc("TRN2", target_bir_lowering=False, num_devices=1)
    arrays, args = {}, []
    for name in _INS:
        a = np.ascontiguousarray(inputs[name])
        arrays[f"in_{name}"] = a
        args.append(nc.dram_tensor(f"in_{name}", a.shape, mybir.dt.from_np(a.dtype), kind="ExternalInput").ap())
    tab = constant_table()
    arrays["in_table"] = tab
    args.append(nc.dram_tensor("in_table", tab.shape, mybir.dt.float32, kind="ExternalInput").ap())
    out = nc.dram_tensor("out_0", (1, S, D), mybir.dt.float32, kind="ExternalOutput").ap()
    peer_encoder(nc, *args, out)
    r = run_bass_kernel_spmd(nc, [arrays], core_ids=[0])
    return r.results[0]["out_0"]
```

```python
import math
import numpy as np
import concourse.bass as bass
from concourse import mybir
from contextlib import ExitStack

D, S, T = 1024, 256, 2
KD = D // 128
FW, AW, NH, HD = 256, 768, 12, 64
NK, PH, KH, TOPK = 128, 8, 64, 16
ALPHA = 2.0 ** 0.25
EPS = 1e-5
NQ, QJ = 4, 32
BODY = 4
C_IOTA, C_BIAS, C_SEQ, C_CHAN, C_INVF, C_IOTA16, C_END = 128, 256, 768, 1792, 2048, 2080, 2304


def peer_encoder(nc, x, c, positions, w_ada, b_ada, w_in, b_in, w_fourier, w_out, b_out, ln1_gain,
                 ln1_bias, w_peer_q, peer_subkeys, peer_u, peer_v, ln2_gain, ln2_bias, table, out):
    f32, i32, u32 = mybir.dt.float32, mybir.dt.int32, mybir.dt.uint32
    f32r, bf16 = mybir.dt.float32r, mybir.dt.bfloat16
    ALU, ACT, AX = mybir.AluOpType, mybir.ActivationFunctionType, mybir.AxisListType
    ds = bass.ds

    x_v = x[0].rearrange("(t p) d -> p t d", p=128)
    out_v = out[0].rearrange("(t p) d -> p t d", p=128)
    pos_v = positions[0].rearrange("(t p) -> p t", p=128)
    ada_v = w_ada[0].rearrange("(k p) n -> p k n", p=128)
    win_v = w_in[0].rearrange("(k p) n -> p k n", p=128)
    wout_v = w_out[0].rearrange("(k p) n -> p k n", p=128)
    wpq_v = w_peer_q[0].rearrange("(k p) n -> p k n", p=128)
    u_v = peer_u[0].rearrange("(i j) d -> i (j d)", i=128)
    v_v = peer_v[0].rearrange("(i j) d -> i (j d)", i=128)
    CHUNKS = [ada_v[:, :, 0:D], ada_v[:, :, D:2 * D], win_v[:, :, 0:1024], win_v[:, :, 1024:2048],
              win_v[:, :, 2048:2560], ada_v[:, :, 2 * D:3 * D], ada_v[:, :, 3 * D:4 * D],
              ada_v[:, :, 4 * D:5 * D], wout_v, wpq_v, ada_v[:, :, 5 * D:6 * D]]
    SH1, SC1, WA, WB, WC, GT1, SH2, SC2, WO, WPQ, GT2 = range(11)
    NSLOT = 3

    with ExitStack() as ctx:
        base = (nc.sbuf_base + 63) // 64 * 64

        def at(name, word, n, dt=f32):
            per = 2 if dt == bf16 else 1
            return nc.alloc_sbuf_tensor_at(name, [128, n * per], dt, offset=base + 4 * word)

        def sem(name):
            return ctx.enter_context(nc.semaphore(name))

        BIG, WORK, CONST, HLO, HSPLIT, XS, UR, G2, SMALL = 0, 24576, 36864, 39168, 41216, 45312, 47360, 51456, 52480
        big = at("big", BIG, NSLOT * 8192)
        work = at("work", WORK, 12288)
        const = at("const", CONST, C_END)
        hTs = at("hTs", HLO, KD * S)
        rows4 = at("rows4", HSPLIT, 4 * D)
        xs = at("xs", XS, T * D)
        uring = at("uring", UR, 4 * D)
        g2s = at("g2s", G2, D)
        cols = at("cols", SMALL, 58)
        csil = at("csil", SMALL + 64, 8)
        modc = at("modc", SMALL + 72, 32)
        pos_i = at("pos_i", SMALL + 104, T, i32)
        pos_f = at("pos_f", SMALL + 112, T)
        stat = at("stat", SMALL + 120, 2 * 6 + 2 + 2)
        rmax = at("rmax", SMALL + 136, 2 * 4)
        rsum = at("rsum", SMALL + 144, 2 * 4)
        iotab = at("iotab", SMALL + 152, 64, bf16)
        uth = at("uth", CONST + 256, 2048, f32r)
        utl = at("utl", HLO, 2048, f32r)
        hth = at("hth", HSPLIT, 2048, f32r)
        htl = at("htl", HSPLIT + 2048, 2048, f32r)
        vring = at("vring", WORK, 4096)
        vlo = at("vlo", WORK, 4096, f32r)
        vhi = at("vhi", WORK + 4096, 2048, f32r)
        whi = at("whi", WORK + 7936, 512, f32r)
        wlo = at("wlo", WORK + 8448, 512, f32r)

        ident = const[:, 0:128]
        iota = const[:, C_IOTA:C_IOTA + 128]
        bias_c = const[:, C_BIAS:C_SEQ].rearrange("p (q k) -> p q k", q=2)
        seq_c = const[:, C_SEQ:C_CHAN].rearrange("p (c k t) -> p c k t", c=2, k=2)
        chan_c = const[:, C_CHAN:C_INVF].rearrange("p (c n) -> p c n", c=2)
        invf = const[:, C_INVF:C_IOTA16]
        x3 = xs[:, :].rearrange("p (t d) -> p t d", t=T)
        hT = hTs[:, :].rearrange("p (k t) -> p k t", k=KD)
        slot3 = [big[:, s * 8192:(s + 1) * 8192].rearrange("p (k n) -> p k n", k=KD) for s in range(NSLOT)]
        wc3 = big[:, (WC % NSLOT) * 8192:(WC % NSLOT) * 8192 + 4096].rearrange("p (k n) -> p k n", k=KD)
        bin_row = work[:, 9728:12032]
        g1s, bout_row = rows4[:, 0:D], rows4[:, D:2 * D]
        gain1, bias1 = rows4[:, 2 * D:3 * D], rows4[:, 3 * D:4 * D]
        rope_cs = work[:, 12032:12160].rearrange("p (c t f) -> p c t f", c=2, t=T)
        rope_w = work[:, 12160:12288].rearrange("p (a t f) -> p a t f", a=2, t=T)
        hn = work[:, 0:2048].rearrange("p (t d) -> p t d", t=T)
        qkv = work[:, 0:4608].rearrange("p (t n) -> p t n", t=T)
        qkT = work[:, 4608:7680].rearrange("p (n t) -> p n t", n=12)
        mixT = work[:, 7680:9728].rearrange("p (k t) -> p k t", k=KD)
        rtmp = work[:, 8192:9728].rearrange("p (a n f) -> p a n f", a=2, f=32)
        prob = work[:, 9728:10752].rearrange("p (b q k) -> p b q k", b=2, q=2)
        probT = work[:, 10752:11776].rearrange("p (b k q) -> p b k q", b=2, k=2)
        fT = uring[:, 0:512].rearrange("p (n t) -> p n t", n=2)
        fw = uring[:, 512:1536].rearrange("p (s n c m) -> p s n c m", s=2, n=2, c=2)
        wfd = uring[:, 1536:1792].rearrange("p (n m) -> p n m", n=2)
        wcs = uring[:, 1792:2304].rearrange("p (n c m) -> p n c m", n=2, c=2)
        rows = uring[0:58, 2304:2432]
        csilB = uring[:, 3072:4096].rearrange("p (k m) -> p k m", k=KD)
        sub = work[:, 0:4096].rearrange("p (t s h k) -> p t s h k", t=T, s=2, h=PH)
        qpT = work[:, 4096:6144].rearrange("p (h t) -> p h t", h=PH)
        dec = work[:, 4096:6144]
        sk = work[:, 6144:7168].rearrange("p (h c) -> p h c", h=PH)
        skT = work[:, 7168:8192].rearrange("p (h k) -> p h k", h=PH)
        cand, subx, candx = work[:, 6144:6400], work[:, 6400:6528], work[:, 6528:6784]
        sv = work[:, 6784:7040].rearrange("p (h s k) -> p h s k", h=PH, s=2)
        si = work[:, 7040:7296].bitcast(u32).rearrange("p (h s k) -> p h s k", h=PH, s=2)
        sif = work[:, 7296:7552].rearrange("p (h s k) -> p h s k", h=PH, s=2)
        OI = work[:, 6144:7168].bitcast(bf16).rearrange("p (b u i) -> p b u i", b=2, u=8)
        OJ = work[:, 7168:7936].bitcast(bf16).rearrange("p (b u c j) -> p b u c j", b=2, u=8, c=3)
        OE = work[:, 9216:9472].bitcast(bf16).rearrange("p (b u j) -> p b u j", b=2, u=8)
        idb = work[:, 9472:9728].bitcast(bf16).rearrange("p (a t) -> p a t", a=2)
        gparts = work[:, 9728:10112].bitcast(bf16).rearrange("p (c t) -> p c t", c=3)
        grest = work[:, 10112:10368]
        tv = work[:, 10368:10624].rearrange("p (t h k) -> p t h k", t=T, h=PH)
        ids = work[:, 10624:11136].rearrange("p (a t n) -> p a t n", a=2, t=T)
        gate = work[:, 11136:11392].rearrange("p (t h k) -> p t h k", t=T, h=PH)
        tpos = work[:, 11392:11520].bitcast(u32)
        posa = work[:, 11520:11648].bitcast(u32)
        posb = work[:, 11648:11776].bitcast(u32)
        gsum = work[:, 11776:11792]
        A4 = [big[:, ((2 + q) % 3) * 8192:((2 + q) % 3 + 1) * 8192] for q in range(NQ)]
        UTH, UTL = (x[:, :].rearrange("p (b k i) -> p b k i", b=2, k=KD) for x in (uth, utl))
        hTH, hTL = (x[:, :].rearrange("p (k t) -> p k t", k=KD) for x in (hth, htl))
        VH = vhi[:, :].rearrange("p (b d) -> p b d", b=2)
        WH, WL = (x[:, :].rearrange("p (b t) -> p b t", b=2) for x in (whi, wlo))
        gain2, bias2 = uring[:, 0:1024], uring[:, 1024:2048]

        P = [ctx.enter_context(nc.psum_tensor(f"P{i}", [128, 512], f32)) for i in range(8)]
        TR, ACTP, GP, Y = P[0:2], P[2], P[3], P[4:8]

        in_table, in_x, in_rows, in_pos = sem("in_table"), sem("in_x"), sem("in_rows"), sem("in_pos")
        in_bcast, in_wf, in_sk, in_ln2 = sem("in_bcast"), sem("in_wf"), sem("in_sk"), sem("in_ln2")
        in_chunk = [sem(f"in_chunk{s}") for s in range(NSLOT)]
        in_u = [sem(f"in_u{s}") for s in range(2)]
        in_v = [sem(f"in_v{s}") for s in range(2)]
        stored = sem("stored")
        pe_rows, cols_ok, csil_ok, csilB_ok = sem("pe_rows"), sem("cols_ok"), sem("csil_ok"), sem("csilB_ok")
        pe_mod, mod_ok = sem("pe_mod"), sem("mod_ok")
        hn_ok, pe_hT, hT_act, hT_dve = sem("hn_ok"), sem("pe_hT"), sem("hT_act"), sem("hT_dve")
        pe_fT, fT_ok, pe_proj, proj_ok = sem("pe_fT"), sem("fT_ok"), sem("pe_proj"), sem("proj_ok")
        pe_gate, gate1_ok, gate2_ok = sem("pe_gate"), sem("gate1_ok"), sem("gate2_ok")
        wf_zero = sem("wf_zero")
        pe_wcs, wcs_ok, pe_fw, fw_ok, pe_mixa = sem("pe_wcs"), sem("wcs_ok"), sem("pe_fw"), sem("fw_ok"), sem("pe_mixa")
        ang_ok, sin_ok, rope_ok, pe_qkT, qkT_ok = sem("ang_ok"), sem("sin_ok"), sem("rope_ok"), sem("pe_qkT"), sem("qkT_ok")
        pe_score, smax_ok, exp_ok, norm_ok = sem("pe_score"), sem("smax_ok"), sem("exp_ok"), sem("norm_ok")
        pe_pT, pT_ok, pe_av, mix_ok = sem("pe_pT"), sem("pT_ok"), sem("pe_av"), sem("mix_ok")
        pe_z = sem("pe_z")
        pe_skT, skT_ok, pe_qp, qp_ok, pe_sub, sub_ok = (sem("pe_skT"), sem("skT_ok"), sem("pe_qp"),
                                                        sem("qp_ok"), sem("pe_sub"), sem("sub_ok"))
        topk_ok, gdiff_ok, gexp_ok, route_ok, pe_idT, idT_ok = (sem("topk_ok"), sem("gdiff_ok"), sem("gexp_ok"),
                                                               sem("route_ok"), sem("pe_idT"), sem("idT_ok"))
        pe_tr0, pe_tr1, uth_ok, utl_ok = sem("pe_tr0"), sem("pe_tr1"), sem("uth_ok"), sem("utl_ok")
        hth_ok, htl_ok = sem("hth_ok"), sem("htl_ok")
        pe_act, gelu_ok = sem("pe_act"), sem("gelu_ok")
        equal_ok, onehot_ok, pe_g, gmul_ok = sem("equal_ok"), sem("onehot_ok"), sem("pe_g"), sem("gmul_ok")
        vh_ok, vl_ok, wh_ok, wl_ok, pe_v = sem("vh_ok"), sem("vl_ok"), sem("wh_ok"), sem("wl_ok"), sem("pe_v")
        sqrt_ok, var_ok = sem("sqrt_ok"), sem("var_ok")
        dve_chain, act_chain = sem("dve_chain"), sem("act_chain")
        fin_ok = sem("fin_ok")

        block = ctx.enter_context(nc.Block())

        def when(eng, s, value):
            if not isinstance(value, int) or value > 0:
                eng.wait_ge(s, value)

        def run_quarter(eng, steps, peel_first, peel_last, each=BODY):
            if peel_first:
                for b in range(each):
                    steps(0, b)
            with eng.Fori(int(peel_first), QJ // each - int(peel_last)) as i:
                for b in range(each):
                    steps(i, b)
            if peel_last:
                for b in range(each):
                    steps(QJ // each - 1, b)

        def chunk_in(eng, n):
            eng.wait_ge(in_chunk[n % NSLOT], 16 * (n // NSLOT + 1))

        @block.sync
        def _(sp):
            sp.dma_start(rows[0:48, :], b_ada[0].rearrange("(a n) -> a n", n=128)).then_inc(in_rows, 16)
            sp.dma_start(rows[48:56, :], c[0].rearrange("(a n) -> a n", n=128)).then_inc(in_rows, 16)
            sp.dma_start(rows[56:58, :], b_in[0, 0:FW].rearrange("(a n) -> a n", n=128)).then_inc(in_rows, 16)
            sp.dma_start(const[:, :], table).then_inc(in_table, 16)
            sp.dma_start(x3, x_v).then_inc(in_x, 16)
            sp.dma_start(pos_i[:, :], pos_v, allow_slow_non_contiguous=True).then_inc(in_pos, 16)
            chunk_read = [(pe_mod, 1), (pe_mod, 2), (pe_proj, 4), (pe_proj, 8), (pe_proj, 10), (pe_gate, 2),
                          (pe_mod, 3), (pe_mod, 4)]
            for n, src in enumerate(CHUNKS):
                if n >= NSLOT:
                    sp.wait_ge(*chunk_read[n - NSLOT])
                dst = wc3 if n == WC else slot3[n % NSLOT]
                sp.dma_start(dst, src).then_inc(in_chunk[n % NSLOT], 16)
            def load_u(n, slot):
                sp.dma_start(uring[:, slot * 2048:(slot + 1) * 2048], u_v[:, ds(n * 2048, 2048)])\
                  .then_inc(in_u[slot], 16)

            def load_v(n, slot):
                sp.dma_start(vring[:, slot * 2048:(slot + 1) * 2048], v_v[:, ds(n * 2048, 2048)])\
                  .then_inc(in_v[slot], 16)

            sp.wait_ge(pe_mixa, 2)
            sp.wait_ge(gate2_ok, 2)
            for n in range(2):
                load_u(n, n)
            with sp.Fori(0, 15) as i:
                for b in range(2):
                    sp.wait_ge(pe_tr1, 4 * i + 2 * b + 2)
                    load_u(2 * i + 2 + b, b)
            sp.wait_ge(topk_ok, 1)
            for n in range(2):
                load_v(n, n)
            def next_u(n, slot, i):
                sp.wait_ge(pe_tr1, 4 * i + 2 * slot + 62)
                load_u(n, slot)

            def next_v(n, slot, i):
                sp.wait_ge(pe_v, 4 * i + 2 * slot - 2)
                load_v(n, slot)

            for b in range(2):
                next_u(32 + b, b, 0)
            with sp.Fori(1, 16) as i:
                for b in range(2):
                    next_u(2 * i + 32 + b, b, i)
                    next_v(2 * i + b, b, i)
            with sp.Fori(16, 32) as i:
                for b in range(2):
                    next_v(2 * i + b, b, i)
            sp.wait_ge(stored, 32)

        @block.gpsimd
        def _(pool):
            pool.memset(wfd, 0.0).then_inc(wf_zero, 1)
            pool.wait_ge(wf_zero, 1)
            for g in range(4):
                h0 = (g % 2) * 64
                pool.dma_start(wfd[h0:h0 + 64, g // 2, h0:h0 + 64], w_fourier[0, g]).then_inc(in_wf, 16)
            for q in range(NQ):
                def steps(i, b):
                    jj = i * BODY + b
                    j = jj + QJ * q
                    pool.wait_ge(wh_ok, j + 1)
                    when(pool, pe_v, j - 1)
                    pool.tensor_tensor(WL[:, b % 2, :], A4[q][:, ds(jj * S, S)], WH[:, b % 2, :].bitcast(f32),
                                       ALU.subtract).then_inc(wl_ok, 1)

                run_quarter(pool, steps, q == 0, False)

        @block.scalar
        def _(act):
            n_chain = [0]

            def link(ins):
                n_chain[0] += 1
                ins.then_inc(act_chain, 1)
                act.wait_ge(act_chain, n_chain[0])

            for dst, src in ((bin_row, b_in[0, FW:]), (bout_row, b_out[0]), (gain1, ln1_gain[0]),
                             (bias1, ln1_bias[0]), (g1s, b_ada[0, 2 * D:3 * D]),
                             (g2s[:, :], b_ada[0, 5 * D:6 * D])):
                act.dma_start(dst, src.partition_broadcast(128)).then_inc(in_bcast, 16)
            act.wait_ge(cols_ok, 1)
            act.activation(csil[:, :], cols[:, 48:56], ACT.Silu).then_inc(csil_ok, 1)

            def root(n):
                act.wait_ge(var_ok, n)
                act.activation(stat[:, 14:15], stat[:, 13:14], ACT.Sqrt).then_inc(sqrt_ok, 1)

            root(1)
            root(2)
            def hT_out(m, turn):
                act.wait_ge(mod_ok, 2 * turn)
                for k in range(4):
                    act.wait_ge(pe_hT, 4 * (turn - 1) + k // 2 + 1)
                    act.activation(hT[:, k, :], P[2 + k // 2][:, (k % 2) * S:(k % 2 + 1) * S], ACT.Identity,
                                   bias=modc[:, m + k:m + k + 1], scale=modc[:, m + 8 + k:m + 9 + k])\
                       .then_inc(hT_act, 1)

            hT_out(0, 1)
            for n in range(2):
                act.wait_ge(pe_fT, n + 1)
                act.activation(fT[:, n, :], P[6 + n][:, 0:S], ACT.Identity, bias=cols[:, 56 + n:57 + n])\
                   .then_inc(fT_ok, 1)
            act.wait_ge(ang_ok, 1)
            act.activation(rope_cs, rope_w, ACT.Sin).then_inc(sin_ok, 1)
            for n in range(2):
                act.wait_ge(pe_wcs, n + 1)
                act.activation(wcs[:, n, :, :], P[6 + n][:, 0:256].rearrange("p (c m) -> p c m", c=2), ACT.Copy)\
                   .then_inc(wcs_ok, 1)
            for s in range(2):
                act.wait_ge(pe_fw, s + 1)
                act.activation(fw[:, s, :, :, :], P[6 + s][:, :].rearrange("p (n c m) -> p n c m", n=2, c=2),
                               ACT.Copy).then_inc(fw_ok, 1)
            for n in range(2):
                act.wait_ge(pe_mixa, n + 1)
                act.activation(mixT[:, n, :], P[6 + n][:, 0:S], ACT.Copy).then_inc(mix_ok, 1)
            for h in range(NH + 1):
                if h < NH:
                    act.wait_ge(smax_ok, h + 1)
                    for q in range(2):
                        act.activation(prob[:, h % 2, q, :], prob[:, h % 2, q, :], ACT.Exp,
                                       bias=rmax[:, 4 * (h % 2) + 2 + q:4 * (h % 2) + 3 + q],
                                       accum_out=rsum[:, 4 * (h % 2) + q:4 * (h % 2) + q + 1]).then_inc(exp_ok, 1)
                if h >= 1:
                    g = h - 1
                    act.wait_ge(pe_pT, g + 1)
                    if g >= 2:
                        act.wait_ge(pe_av, g - 1)
                    act.activation(probT[:, g % 2, :, :], P[2 + g % 2][:, :].rearrange("p (k q) -> p k q", k=2),
                                   ACT.Copy).then_inc(pT_ok, 1)
                    if g % 2:
                        act.wait_ge(pe_av, g + 1)
                        act.activation(mixT[:, 2 + g // 2, :], P[4 + (g // 2) % 2][:, 0:S], ACT.Copy)\
                           .then_inc(mix_ok, 1)
            act.wait_ge(pe_av, NH)
            act.dma_start(sk, peer_subkeys[0].rearrange("h s k c -> k h s c")).then_inc(in_sk, 16)
            for n in range(2):
                act.wait_ge(pe_skT, n + 1)
                act.activation(skT[:, 4 * n:4 * n + 4, :], P[4 + n][:, :].rearrange("p (h k) -> p h k", h=4),
                               ACT.Copy).then_inc(skT_ok, 1)
            for n in range(3, 7):
                root(n)
            hT_out(16, 2)
            for n in range(4):
                act.wait_ge(pe_qp, n + 1)
                act.activation(qpT[:, 2 * n:2 * n + 2, :], P[(6, 7, 0, 1)[n]][:, :].rearrange("p (h t) -> p h t", h=2),
                               ACT.Copy).then_inc(qp_ok, 1)
            for n in range(8):
                t, s, hh = n // 4, n // 2 % 2, n % 2
                act.wait_ge(pe_sub, n + 1)
                act.activation(sub[:, t, s, 4 * hh:4 * hh + 4, :],
                               P[(2, 3, 4, 5, 6, 7, 0, 1)[n]][:, :].rearrange("p (h k) -> p h k", h=4), ACT.Copy)\
                   .then_inc(sub_ok, 1)

            for k in range(KD):
                act.wait_ge(hT_act, 8)
                act.wait_ge(hT_dve, 8)
                act.activation(hTH[:, k, :], hT[:, k, :], ACT.Copy).then_inc(hth_ok, 1)

            def ut_high(b, j):
                for half, done in ((0, pe_tr0), (1, pe_tr1)):
                    act.wait_ge(done, j + 1)
                    when(act, pe_act, j - 1)
                    act.activation(UTH[:, b, 4 * half:4 * half + 4, :],
                                   TR[half][:, :].rearrange("p (k i) -> p k i", k=4), ACT.Copy).then_inc(uth_ok, 1)

            act.wait_ge(gate2_ok, 2)
            ut_high(0, 0)
            for q in range(NQ + 2):
                def steps(i, b):
                    jj = i * BODY + b
                    if q < NQ and not (isinstance(i, int) and jj + QJ * q == NK - 1):
                        ut_high((b + 1) % 2, jj + 1 + QJ * q)
                    if q >= 2:
                        jv = jj + QJ * (q - 2)
                        act.wait_ge(in_v[b // 2], 16 * (i + QJ // BODY * (q - 2) + 1))
                        when(act, pe_v, jv - 1)
                        act.activation(VH[:, b % 2, :], vring[:, b * D:b * D + D], ACT.Copy).then_inc(vh_ok, 1)
                        act.wait_ge(gmul_ok, QJ * (q - 1))
                        act.activation(WH[:, b % 2, :], A4[q - 2][:, ds(jj * S, S)], ACT.Copy).then_inc(wh_ok, 1)
                    if q < NQ:
                        j = jj + QJ * q
                        act.wait_ge(pe_act, j + 1)
                        if q == 3:
                            act.wait_ge(wl_ok, QJ)
                        act.activation(A4[q][:, ds(jj * S, S)], ACTP[:, 0:S], ACT.Gelu).then_inc(gelu_ok, 1)

                run_quarter(act, steps, q in (0, 2), q == NQ - 1)
                if q == 0:
                    act.wait_ge(gdiff_ok, 1)
                    act.activation(gate, gate, ACT.Exp).then_inc(gexp_ok, 1)
            act.wait_ge(pe_tr1, 4 * QJ)
            for dst, src in ((gain2, ln2_gain[0]), (bias2, ln2_bias[0])):
                act.dma_start(dst, src.partition_broadcast(128)).then_inc(in_ln2, 16)
            for t in range(T):
                root(7 + t)
                act.wait_ge(fin_ok, t + 1)
                act.dma_start(out_v[:, t, :], x3[:, t, :]).then_inc(stored, 16)
            act.wait_ge(stored, 32)

        @block.vector
        def _(dve):
            count = {}

            def link(ins, signal=None):
                s = dve_chain if signal is None else signal
                count[id(s)] = count.get(id(s), 0) + 1
                ins.then_inc(s, 1)
                dve.wait_ge(s, count[id(s)])

            roots = [0]

            def normalise(dst, src):
                for n in range(2):
                    last = dve.bn_stats(stat[:, 6 * n:6 * n + 6], src[:, 512 * n:512 * n + 512])
                    link(last)
                link(dve.bn_aggr(stat[:, 12:14], stat[:, 0:12].rearrange("p (a b) -> p a b", a=2)))
                roots[0] += 1
                link(dve.tensor_scalar(stat[:, 13:14], stat[:, 13:14], EPS, None, ALU.add), var_ok)
                dve.wait_ge(sqrt_ok, roots[0])
                link(dve.reciprocal(stat[:, 15:16], stat[:, 14:15]))
                return dve.tensor_scalar(dst, src, stat[:, 12:13], stat[:, 15:16], ALU.subtract, ALU.mult)

            def transposed_h(m, turn):
                for k in range(4, 8):
                    dve.wait_ge(pe_hT, 4 * (turn - 1) + k // 2 + 1)
                    dve.tensor_scalar(hT[:, k, :], P[2 + k // 2][:, (k % 2) * S:(k % 2 + 1) * S],
                                      modc[:, m + 8 + k:m + 9 + k], modc[:, m + k:m + k + 1],
                                      ALU.mult, ALU.add).then_inc(hT_dve, 1)

            def modulation(chunk, m, one, n):
                dve.wait_ge(pe_mod, n)
                link(dve.scalar_tensor_tensor(modc[:, m:m + 8], P[1 - m // 8 % 2][:, m:m + 8], one,
                                              cols[:, 8 * chunk:8 * chunk + 8], ALU.add, ALU.add), mod_ok)

            dve.wait_ge(pe_rows, 1)
            link(dve.tensor_copy(cols[:, :], P[0][:, 0:58]), cols_ok)
            dve.wait_ge(csil_ok, 1)
            dve.tensor_copy(csilB, csil[:, :].unsqueeze(2).to_broadcast([128, 8, 128])).then_inc(csilB_ok, 1)
            dve.wait_ge(in_x, 16)
            for t in range(T):
                link(normalise(hn[:, t, :], x3[:, t, :]), hn_ok)
            dve.wait_ge(in_pos, 16)
            dve.wait_ge(in_table, 16)
            link(dve.tensor_copy(pos_f[:, :], pos_i[:, :]))
            for t in range(T):
                for a in range(2):
                    link(dve.tensor_scalar(rope_w[:, a, t, :], invf, pos_f[:, t:t + 1], None, ALU.mult))
            TURN = 2.0 * math.pi
            C1 = 6.28125
            C2 = float(np.float32(np.round((TURN - C1) * 2 ** 21) / 2 ** 21))
            C3 = float(np.float32(TURN - C1 - C2))
            ROUND = 12582912.0
            for a, lead in ((0, 0.25), (1, 0.0)):
                w, n = rope_w[:, a, :, :], rope_cs[:, a, :, :]
                link(dve.tensor_scalar(n, w, 1.0 / TURN, lead, ALU.mult, ALU.add))
                link(dve.tensor_scalar(n, n, ROUND, None, ALU.add))
                link(dve.tensor_scalar(n, n, ROUND, None, ALU.subtract))
                for part in (C1, C2, C3):
                    link(dve.scalar_tensor_tensor(w, n, -part, w, ALU.mult, ALU.add))
                if a == 0:
                    link(dve.tensor_scalar(w, w, math.pi / 2, None, ALU.add))
                lim = 3.1415925
                link(dve.tensor_scalar(w, w, -lim, lim, ALU.max, ALU.min))
            link(dve.tensor_copy(pos_f[:, :], pos_i[:, :]), ang_ok)
            modulation(0, 0, 0.0, 1)
            modulation(1, 8, 1.0, 2)
            transposed_h(0, 1)
            dve.wait_ge(in_bcast, 16 * 6)
            dve.wait_ge(hT_dve, 4)
            dve.wait_ge(pe_hT, 4)
            for g, (t, c0, n) in enumerate(GROUPS):
                dve.wait_ge(pe_proj, g + 1)
                dve.tensor_tensor(qkv[:, t, c0:c0 + n], P[2 + g % 4][:, 0:n], bin_row[:, c0:c0 + n], ALU.add)\
                   .then_inc(proj_ok, 1)
            for n in range(2):
                dve.wait_ge(pe_gate, n + 1)
                dve.scalar_tensor_tensor(g1s[:, 512 * n:512 * n + 512], P[6 + n][:, :], 1.0,
                                         g1s[:, 512 * n:512 * n + 512], ALU.add, ALU.add).then_inc(gate1_ok, 1)
            dve.wait_ge(proj_ok, len(GROUPS))
            dve.wait_ge(sin_ok, 1)
            for t in range(T):
                qk = qkv[:, t, 0:2 * AW].rearrange("p (n two f) -> p n two f", two=2, f=32)
                cs = rope_cs[:, 0, t, :].unsqueeze(1).to_broadcast([128, 24, 32])
                sn = rope_cs[:, 1, t, :].unsqueeze(1).to_broadcast([128, 24, 32])
                t1, t2 = qk[:, :, 0, :], qk[:, :, 1, :]
                link(dve.tensor_tensor(rtmp[:, 0], t1, sn, ALU.mult))
                link(dve.tensor_tensor(rtmp[:, 1], t2, sn, ALU.mult))
                link(dve.tensor_tensor(t1, t1, cs, ALU.mult))
                link(dve.tensor_tensor(t2, t2, cs, ALU.mult))
                link(dve.tensor_tensor(t1, t1, rtmp[:, 1], ALU.subtract))
                link(dve.tensor_tensor(t2, t2, rtmp[:, 0], ALU.add), rope_ok)
            for b in range(6):
                dve.wait_ge(pe_qkT, b + 1)
                dve.tensor_copy(qkT[:, 2 * b:2 * b + 2, :], P[2 + b % 4][:, :].rearrange("p (n t) -> p n t", n=2))\
                   .then_inc(qkT_ok, 1)
            modulation(3, 16, 0.0, 3)
            modulation(4, 24, 1.0, 4)
            def score_max(h):
                dve.wait_ge(pe_score, h + 1)
                if h >= 2:
                    dve.wait_ge(pe_pT, h - 1)
                r = rmax[:, 4 * (h % 2):4 * (h % 2) + 4]
                for q in range(2):
                    link(dve.tensor_tensor_reduce(out=prob[:, h % 2, q, :], in0=P[h % 2][:, q * S:(q + 1) * S],
                                                  in1=bias_c[:, q, :], scale=HD ** -0.5, scalar=-3.0e38,
                                                  op0=ALU.add, op1=ALU.max, accum_out=r[:, q:q + 1]))
                link(dve.tensor_scalar(r[:, 2:4], r[:, 0:2], -1.0, None, ALU.mult), smax_ok)

            def over_sum(h):
                dve.wait_ge(exp_ok, 2 * h + 2)
                r = rsum[:, 4 * (h % 2):4 * (h % 2) + 4]
                link(dve.reciprocal(r[:, 2:4], r[:, 0:2]))
                for q in range(2):
                    dve.tensor_scalar(prob[:, h % 2, q, :], prob[:, h % 2, q, :], r[:, 2 + q:3 + q], None,
                                      ALU.mult).then_inc(norm_ok, 1)

            score_max(0)
            for h in range(NH):
                if h + 1 < NH:
                    score_max(h + 1)
                over_sum(h)
            for t in range(T):
                for n in range(2):
                    s = slice(512 * n, 512 * n + 512)
                    dve.wait_ge(pe_z, 2 * t + n + 1)
                    link(dve.tensor_tensor(hn[:, t, s], P[(6, 7, 0, 1)[2 * t + n]][:, :], bout_row[:, s], ALU.add))
                link(dve.tensor_tensor(hn[:, t, :], hn[:, t, :], g1s[:, :], ALU.mult))
                link(dve.scalar_tensor_tensor(x3[:, t, :], x3[:, t, :], ALPHA, hn[:, t, :], ALU.mult, ALU.add))
                link(normalise(x3[:, t, :], x3[:, t, :]))
                link(dve.tensor_tensor(x3[:, t, :], x3[:, t, :], gain1, ALU.mult))
                link(dve.tensor_tensor(x3[:, t, :], x3[:, t, :], bias1, ALU.add))
                link(normalise(hn[:, t, :], x3[:, t, :]), hn_ok)
            transposed_h(16, 2)
            for n in range(2):
                dve.wait_ge(pe_gate, n + 3)
                dve.scalar_tensor_tensor(g2s[:, 512 * n:512 * n + 512], P[2 + n][:, :], 1.0,
                                         g2s[:, 512 * n:512 * n + 512], ALU.add, ALU.add).then_inc(gate2_ok, 1)

            for k in range(KD):
                dve.wait_ge(hth_ok, k + 1)
                dve.tensor_tensor(hTL[:, k, :], hT[:, k, :], hTH[:, k, :].bitcast(f32), ALU.subtract)\
                   .then_inc(htl_ok, 1)
            dve.wait_ge(htl_ok, KD)

            def ut_low(b, j):
                for half in range(2):
                    dve.wait_ge(uth_ok, 2 * j + half + 1)
                    when(dve, pe_act, j - 1)
                    k = slice(4 * half, 4 * half + 4)
                    dve.tensor_tensor(UTL[:, b, k, :], TR[half][:, :].rearrange("p (k i) -> p k i", k=4),
                                      UTH[:, b, k, :].bitcast(f32), ALU.subtract).then_inc(utl_ok, 1)

            def top16(values, scratch, best, where):
                link(dve.max(best[:, 0:8], values))
                link(dve.max_index(where[:, 0:8], best[:, 0:8], values))
                link(dve.match_replace(scratch, best[:, 0:8], values, -3.0e38))
                link(dve.max(best[:, 8:16], scratch))
                link(dve.max_index(where[:, 8:16], best[:, 8:16], scratch))

            def head_keys(t, h):
                for s in range(2):
                    top16(sub[:, t, s, h, :], subx, sv[:, h, s, :], si[:, h, s, :])

            def head_pairs(t, h):
                c3 = cand.rearrange("p (a b) -> p a b", a=TOPK)
                link(dve.tensor_tensor(c3, sv[:, h, 0, :].unsqueeze(2).to_broadcast([128, TOPK, TOPK]),
                                       sv[:, h, 1, :].unsqueeze(1).to_broadcast([128, TOPK, TOPK]), ALU.add))
                top16(cand, candx, tv[:, t, h, :], tpos[:, h * TOPK:(h + 1) * TOPK])

            def key_ids(t):
                link(dve.tensor_copy(sif, si))
                link(dve.tensor_scalar(posa, tpos, 4, None, ALU.logical_shift_right))
                link(dve.tensor_scalar(posb, tpos, 15, None, ALU.bitwise_and))
                i16 = iota[:, 0:16].unsqueeze(1).to_broadcast([128, 128, 16])
                d3 = dec.rearrange("p (n a) -> p n a", a=16)
                d4 = dec.rearrange("p (h k a) -> p h k a", h=PH, k=TOPK)
                for s, where in ((0, posa), (1, posb)):
                    link(dve.tensor_tensor(d3, where.unsqueeze(2).to_broadcast([128, 128, 16]), i16, ALU.is_equal))
                    link(dve.tensor_tensor(d4, d4, sif[:, :, s, :].unsqueeze(2).to_broadcast([128, PH, TOPK, 16]),
                                           ALU.mult))
                    link(dve.tensor_reduce(ids[:, s, t, :], d3, AX.X, ALU.add))

            dve.wait_ge(sub_ok, 8)
            ut_low(0, 0)
            for j in range(QJ):
                ut_low((j + 1) % 2, j + 1)
                t, h = j // 16, j % 16 // 2
                if j % 2 == 0:
                    head_keys(t, h)
                else:
                    head_pairs(t, h)
                if j % 16 == 15:
                    key_ids(t)
            link(dve.tensor_tensor(gate, tv, tv[:, :, :, 0:1].to_broadcast([128, T, PH, TOPK]), ALU.subtract), topk_ok)
            link(dve.memset(gsum, 0.0), gdiff_ok)
            dve.wait_ge(gexp_ok, 1)
            g2 = gsum.rearrange("p (t h) -> p t h", t=T)
            link(dve.tensor_reduce(g2, gate, AX.X, ALU.add))
            link(dve.reciprocal(gsum, gsum))
            link(dve.tensor_tensor(gate, gate, g2.unsqueeze(3).to_broadcast([128, T, PH, TOPK]), ALU.mult), route_ok)
            link(dve.tensor_copy(iotab[:, :], iota))
            for t in range(T):
                dve.wait_ge(pe_idT, t + 1)
                tok = slice(128 * t, 128 * t + 128)
                link(dve.tensor_copy(idb[:, :, tok], GP[:, 0:256].rearrange("p (a t) -> p a t", a=2)))
                link(dve.tensor_copy(grest[:, tok], GP[:, 256:384]), idT_ok)
            for n in range(3):
                link(dve.tensor_copy(gparts[:, n, :], grest))
                if n < 2:
                    link(dve.tensor_tensor(grest, grest, gparts[:, n, :], ALU.subtract))

            def onehots(q, g, b, n):
                by_i = idb[:, 0, ds(g * 8, 8)].unsqueeze(2).to_broadcast([128, 8, 128])
                by_j = idb[:, 1, ds(g * 8, 8)].unsqueeze(2).to_broadcast([128, 8, QJ])
                dve.tensor_tensor(OE[:, b], iotab[:, QJ * q:QJ * q + QJ].unsqueeze(1).to_broadcast([128, 8, QJ]),
                                  by_j, ALU.is_equal).then_inc(equal_ok, 1)
                dve.tensor_tensor(OI[:, b], iotab[:, :].unsqueeze(1).to_broadcast([128, 8, 128]), by_i, ALU.is_equal)
                dve.wait_ge(equal_ok, n + 1)
                dve.tensor_tensor(OJ[:, b], OE[:, b].unsqueeze(2).to_broadcast([128, 8, 3, QJ]),
                                  gparts[:, :, ds(g * 8, 8)].rearrange("p c u -> p u c").unsqueeze(3)
                                  .to_broadcast([128, 8, 3, QJ]), ALU.mult).then_inc(onehot_ok, 1)

            def apply_gates(q, g, n):
                dve.wait_ge(pe_g, n + 1)
                dve.wait_ge(gelu_ok, QJ * (q + 1))
                a = A4[q].rearrange("p (j t) -> p j t", t=S)[:, :, ds(g * 8, 8)]
                dve.tensor_tensor(a, a, GP[:, 0:256].rearrange("p (u j) -> p j u", u=8), ALU.mult)\
                   .then_inc(gmul_ok, 1)

            for q in range(1, NQ + 2):
                def steps(i, b):
                    jj = i * BODY + b
                    if q <= NQ:
                        onehots(q - 1, jj, b % 2, jj + QJ * (q - 1))
                    if q < NQ and not (isinstance(i, int) and jj + QJ * q == NK - 1):
                        ut_low((b + 1) % 2, jj + 1 + QJ * q)
                    if q >= 2:
                        dve.wait_ge(vh_ok, jj + QJ * (q - 2) + 1)
                        v = slice(b * D, b * D + D)
                        dve.tensor_tensor(vlo[:, v], vring[:, v], VH[:, b % 2, :].bitcast(f32), ALU.subtract)\
                           .then_inc(vl_ok, 1)
                    if q <= NQ:
                        apply_gates(q - 1, jj, jj + QJ * (q - 1))

                run_quarter(dve, steps, False, q == NQ - 1)
            dve.wait_ge(in_ln2, 32)
            dve.wait_ge(pe_v, 4 * QJ)
            for t in range(T):
                ys = big[:, 1024 * t:1024 * t + 1024]
                for n in range(2):
                    s = slice(512 * n, 512 * n + 512)
                    link(dve.tensor_tensor(ys[:, s], Y[2 * t + n][:, :], g2s[:, s], ALU.mult))
                link(dve.scalar_tensor_tensor(x3[:, t, :], x3[:, t, :], ALPHA, ys, ALU.mult, ALU.add))
                link(normalise(x3[:, t, :], x3[:, t, :]))
                link(dve.tensor_tensor(x3[:, t, :], x3[:, t, :], gain2, ALU.mult))
                link(dve.tensor_tensor(x3[:, t, :], x3[:, t, :], bias2, ALU.add), fin_ok)

        @block.tensor
        def _(pe):
            mm = pe.matmul

            def transpose(dst, src):
                return pe.transpose(dst, src, ident[0:src.shape[0], 0:src.shape[0]])

            def mod_columns(n, m):
                chunk_in(pe, n)
                for a in range(8):
                    for k in range(KD):
                        last = mm(P[1 - m // 8 % 2][:, m + a:m + a + 1], slot3[n % NSLOT][:, k, a * 128:a * 128 + 128],
                                  csil[:, k:k + 1], start=(k == 0), stop=(k == KD - 1))
                last.then_inc(pe_mod, 1)

            def gate_rows(n, banks):
                chunk_in(pe, n)
                for a in range(2):
                    for k in range(KD):
                        last = mm(banks[a][:, :], csilB[:, k, :], slot3[n % NSLOT][:, k, 512 * a:512 * a + 512],
                                  start=(k == 0), stop=(k == KD - 1))
                    last.then_inc(pe_gate, 1)

            def h_transposes(turn):
                pe.wait_ge(hn_ok, 2 * turn)
                for b in range(4):
                    for kk in range(2):
                        for t in range(T):
                            k = 2 * b + kk
                            last = transpose(P[2 + b][:, kk * S + t * 128:kk * S + t * 128 + 128],
                                             hn[:, t, k * 128:k * 128 + 128])
                    last.then_inc(pe_hT, 1)

            pe.wait_ge(in_table, 16)
            pe.wait_ge(in_rows, 48)
            transpose(P[0][:, 0:58], rows).then_inc(pe_rows, 1)
            pe.wait_ge(csil_ok, 1)
            mod_columns(SH1, 0)
            mod_columns(SC1, 8)
            h_transposes(1)
            pe.wait_ge(hT_act, 4)
            pe.wait_ge(hT_dve, 4)
            chunk_in(pe, WA)
            for n in range(2):
                for k in range(KD):
                    last = mm(P[6 + n][:, 0:S], slot3[WA % NSLOT][:, k, n * 128:n * 128 + 128], hT[:, k, :],
                              start=(k == 0), stop=(k == KD - 1))
                last.then_inc(pe_fT, 1)
            for g, (t, c0, n) in enumerate(GROUPS):
                w, col, n_chunk = ((slot3[WA % NSLOT], c0 + FW, WA) if c0 < 768 else
                                   (slot3[WB % NSLOT], c0 - 768, WB) if c0 < 1792 else (wc3, c0 - 1792, WC))
                chunk_in(pe, n_chunk)
                if g >= 4:
                    pe.wait_ge(proj_ok, g - 3)
                for k in range(KD):
                    last = mm(P[2 + g % 4][:, 0:n], hT[:, k, t * 128:t * 128 + 128], w[:, k, col:col + n],
                              start=(k == 0), stop=(k == KD - 1))
                last.then_inc(pe_proj, 1)
            pe.wait_ge(csilB_ok, 1)
            pe.wait_ge(fT_ok, 2)
            gate_rows(GT1, (P[6], P[7]))
            pe.wait_ge(mod_ok, 2)
            pe.wait_ge(gate1_ok, 2)
            mod_columns(SH2, 16)
            mod_columns(SC2, 24)
            pe.wait_ge(in_wf, 64)
            for n in range(2):
                for cs in range(2):
                    last = mm(P[6 + n][:, cs * 128:cs * 128 + 128], chan_c[:, cs, :], wfd[:, n, :], start=True, stop=True)
                last.then_inc(pe_wcs, 1)
            pe.wait_ge(wcs_ok, 2)
            for s in range(2):
                for n in range(2):
                    last = mm(P[6 + s][:, n * 256:n * 256 + 256], fT[:, n, s * 128:s * 128 + 128],
                              wcs[:, n, :, :].rearrange("p c m -> p (c m)"), start=True, stop=True)
                last.then_inc(pe_fw, 1)
            pe.wait_ge(fw_ok, 2)
            for n in range(2):
                for i, (cs, s) in enumerate(((0, 0), (0, 1), (1, 0), (1, 1))):
                    last = mm(P[6 + n][:, 0:S], fw[:, s, n, cs, :], seq_c[:, cs, s, :], start=(i == 0), stop=(i == 3))
                last.then_inc(pe_mixa, 1)
            pe.wait_ge(rope_ok, 2)
            for b in range(6):
                if b >= 4:
                    pe.wait_ge(qkT_ok, b - 3)
                for kk in range(2):
                    for t in range(T):
                        n = 2 * b + kk
                        last = transpose(P[2 + b % 4][:, kk * S + t * 128:kk * S + t * 128 + 128],
                                         qkv[:, t, n * 128:n * 128 + 128])
                last.then_inc(pe_qkT, 1)

            def scores(h):
                p0 = (h % 2) * 64
                if h >= 2:
                    pe.wait_ge(smax_ok, h - 1)
                for q in range(2):
                    last = mm(P[h % 2][:, q * S:(q + 1) * S], qkT[p0:p0 + 64, h // 2, q * 128:q * 128 + 128],
                              qkT[p0:p0 + 64, 6 + h // 2, :], start=True, stop=True)
                last.then_inc(pe_score, 1)

            def attend(h):
                pe.wait_ge(norm_ok, 2 * h + 2)
                if h >= 2:
                    pe.wait_ge(pT_ok, h - 1)
                for k in range(2):
                    for q in range(2):
                        last = transpose(P[2 + h % 2][:, k * S + q * 128:k * S + q * 128 + 128],
                                         prob[:, h % 2, q, k * 128:k * 128 + 128])
                last.then_inc(pe_pT, 1)

            def values(h):
                p0 = (h % 2) * 64
                pe.wait_ge(pT_ok, h + 1)
                if h >= 4:
                    pe.wait_ge(mix_ok, 2 + h // 2 - 1)
                for k in range(2):
                    last = mm(P[4 + (h // 2) % 2][p0:p0 + 64, 0:S], qkv[:, k, 2 * AW + h * HD:2 * AW + h * HD + HD],
                              probT[:, h % 2, k, :], start=(k == 0), stop=(k == 1))
                last.then_inc(pe_av, 1)

            pe.wait_ge(qkT_ok, 6)
            pe.wait_ge(mod_ok, 4)
            scores(0)
            scores(1)
            for h in range(NH):
                attend(h)
                if h + 2 < NH:
                    scores(h + 2)
                values(h)
            pe.wait_ge(mix_ok, 8)
            pe.wait_ge(smax_ok, NH)
            chunk_in(pe, WO)
            for t in range(T):
                for n in range(2):
                    for k in range(KD):
                        last = mm(P[(6, 7, 0, 1)[2 * t + n]][:, :], mixT[:, k, t * 128:t * 128 + 128],
                                  slot3[WO % NSLOT][:, k, 512 * n:512 * n + 512], start=(k == 0), stop=(k == KD - 1))
                    last.then_inc(pe_z, 1)
            pe.wait_ge(in_sk, 16)
            for n in range(2):
                for h in range(4):
                    last = transpose(P[4 + n][:, h * 128:h * 128 + 128], sk[:, 4 * n + h, :])
                last.then_inc(pe_skT, 1)
            pe.wait_ge(skT_ok, 2)
            h_transposes(2)
            pe.wait_ge(hT_act, 8)
            pe.wait_ge(hT_dve, 8)
            chunk_in(pe, WPQ)
            for n in range(4):
                for hh in range(2):
                    h = 2 * n + hh
                    for k in range(KD):
                        last = mm(P[(6, 7, 0, 1)[n]][:, hh * S:hh * S + S],
                                  slot3[WPQ % NSLOT][:, k, h * 128:h * 128 + 128], hT[:, k, :],
                                  start=(k == 0), stop=(k == KD - 1))
                last.then_inc(pe_qp, 1)
            pe.wait_ge(qp_ok, 4)
            gate_rows(GT2, (P[2], P[3]))
            pe.wait_ge(gate2_ok, 2)
            for n in range(8):
                t, s, hh = n // 4, n // 2 % 2, n % 2
                for h in range(4 * hh, 4 * hh + 4):
                    last = mm(P[(2, 3, 4, 5, 6, 7, 0, 1)[n]][:, (h % 4) * 128:(h % 4) * 128 + 128],
                              qpT[64 * s:64 * s + 64, h, t * 128:t * 128 + 128], skT[64 * s:64 * s + 64, h, :],
                              start=True, stop=True)
                last.then_inc(pe_sub, 1)
            pe.wait_ge(sub_ok, 8)

            def u_transposes(slot, j, turn):
                if slot % 2 == 0:
                    pe.wait_ge(in_u[slot // 2], turn)
                for half, done in ((0, pe_tr0), (1, pe_tr1)):
                    when(pe, utl_ok, 2 * j + half - 1)
                    for k in range(4):
                        kk = 4 * half + k
                        last = transpose(TR[half][:, k * 128:k * 128 + 128],
                                         uring[:, slot * D + kk * 128:slot * D + kk * 128 + 128])
                    last.then_inc(done, 1)

            def u_product(b, j):
                pe.wait_ge(uth_ok, 2 * j + 2)
                when(pe, gelu_ok, j)
                for k in range(KD):
                    mm(ACTP[:, 0:S], UTH[:, b, k, :], hTH[:, k, :], start=(k == 0), stop=False)
                    mm(ACTP[:, 0:S], UTH[:, b, k, :], hTL[:, k, :], start=False, stop=False)
                pe.wait_ge(utl_ok, 2 * j + 2)
                for k in range(KD):
                    last = mm(ACTP[:, 0:S], UTL[:, b, k, :], hTH[:, k, :], start=False, stop=(k == KD - 1))
                last.then_inc(pe_act, 1)

            def gates(b, n):
                pe.wait_ge(onehot_ok, n + 1)
                when(pe, gmul_ok, n)
                for u in range(8):
                    for part in range(3):
                        last = mm(GP[:, u * QJ:u * QJ + QJ], OI[:, b, u, :], OJ[:, b, u, part, :],
                                  start=(part == 0), stop=(part == 2))
                last.then_inc(pe_g, 1)

            def v_product(slot, j, first=False, final=False):
                pe.wait_ge(wh_ok, j + 1)
                b = slot % 2

                def one(w, v, v0, start, stop):
                    for t in range(T):
                        for n in range(2):
                            last = mm(Y[2 * t + n][:, :], w[:, b, t * 128:t * 128 + 128],
                                      v[:, v0 + 512 * n:v0 + 512 * n + 512], start=start, stop=stop)
                    return last

                one(WH, vhi, b * D, first, False)
                pe.wait_ge(wl_ok, j + 1)
                one(WL, vhi, b * D, False, False)
                pe.wait_ge(vl_ok, j + 1)
                one(WH, vlo, slot * D, False, final).then_inc(pe_v, 1)

            pe.wait_ge(hth_ok, KD)
            pe.wait_ge(htl_ok, KD)
            u_transposes(0, 0, 16)
            for q in range(NQ + 2):
                u_on, g_on, v_on = q < NQ, 1 <= q < NQ + 1, q >= 2

                def steps(i, b):
                    jj = i * BODY + b
                    if u_on and not (q == NQ - 1 and isinstance(i, int) and jj == QJ - 1):
                        u_transposes((b + 1) % BODY, jj + 1 + QJ * q, 16 * (i + QJ // BODY * q + 1 + (b == BODY - 1)))
                    if u_on:
                        u_product(b % 2, jj + QJ * q)
                    if g_on:
                        gates(b % 2, jj + QJ * (q - 1))
                    if v_on:
                        v_product(b, jj + QJ * (q - 2), first=q == 2 and isinstance(i, int) and jj == 0,
                                  final=q == NQ + 1 and isinstance(i, int) and jj == QJ - 1)

                head = q <= 2
                tail = q in (NQ - 1, NQ + 1)
                if q == 1:
                    pe.wait_ge(route_ok, 1)
                    for t in range(T):
                        if t:
                            pe.wait_ge(idT_ok, t)
                        for a in range(3):
                            src = ids[:, a, t, :] if a < 2 else gate[:, t, :, :].rearrange("p h k -> p (h k)")
                            last = transpose(GP[:, a * 128:a * 128 + 128], src)
                        last.then_inc(pe_idT, 1)
                    pe.wait_ge(idT_ok, 2)
                run_quarter(pe, steps, head, tail)


GROUPS = [(t, c, 384) for c in (0, 384) for t in range(2)] + \
         [(t, c, 512) for c in (768, 1280) for t in range(2)] + [(t, 1792, 512) for t in range(2)]


def constant_table():
    tab = np.zeros((128, C_END), np.float64)
    p = np.arange(128)
    tab[:, 0:128] = np.eye(128)
    tab[:, C_IOTA:C_IOTA + 128] = np.arange(128)
    q = p[:, None, None] + 128 * np.arange(2)[None, :, None]
    off = np.arange(S)[None, None, :] - q
    n = np.zeros(off.shape)
    for window, dil in ((128, 1), (512, 4), (2048, 16)):
        n += (off % dil == 0) & (np.abs(off) <= window // 2)
    tab[:, C_BIAS:C_SEQ] = (np.where(n > 0, np.log(np.maximum(n, 1)), -1e30) * HD ** 0.5).reshape(128, -1)
    s = p[:, None, None] + 128 * np.arange(2)[None, :, None]
    ang = 2 * np.pi * ((s * np.arange(S)[None, None, :]) % S) / S
    norm = 1.0 / math.sqrt(S * 64)
    tab[:, C_SEQ:C_CHAN] = np.stack([np.cos(ang) * norm, -np.sin(ang) * norm], 1).reshape(128, -1)
    c = np.arange(64)
    ang = 2 * np.pi * (np.outer(c, c) % 64) / 64
    for k, m in enumerate((np.cos(ang), np.sin(ang))):
        for g in range(2):
            tab[64 * g:64 * g + 64, C_CHAN + 128 * k + 64 * g:C_CHAN + 128 * k + 64 * g + 64] = m
    inv = (np.float32(10000.0) ** (-np.arange(32, dtype=np.float32) / np.float32(32))).astype(np.float32)
    tab[:, C_INVF:C_INVF + 32] = inv
    return tab.astype(np.float32)


_INS = ["x", "c", "positions", "w_ada", "b_ada", "w_in", "b_in", "w_fourier", "w_out", "b_out", "ln1_gain",
        "ln1_bias", "w_peer_q", "peer_subkeys", "peer_u", "peer_v", "ln2_gain", "ln2_bias"]


def kernel(**inputs):
    import concourse.bacc as bacc
    from concourse.bass_utils import run_bass_kernel_spmd

    nc = bacc.Bacc("TRN2", target_bir_lowering=False, num_devices=1)
    arrays, args = {}, []
    for name in _INS:
        a = np.ascontiguousarray(inputs[name])
        arrays[f"in_{name}"] = a
        args.append(nc.dram_tensor(f"in_{name}", a.shape, mybir.dt.from_np(a.dtype), kind="ExternalInput").ap())
    tab = constant_table()
    arrays["in_table"] = tab
    args.append(nc.dram_tensor("in_table", tab.shape, mybir.dt.float32, kind="ExternalInput").ap())
    out = nc.dram_tensor("out_0", (1, S, D), mybir.dt.float32, kind="ExternalOutput").ap()
    peer_encoder(nc, *args, out)
    r = run_bass_kernel_spmd(nc, [arrays], core_ids=[0])
    return r.results[0]["out_0"]
```

```python
import math
import numpy as np
import concourse.bass as bass
from concourse import mybir
from contextlib import ExitStack

D, S, T = 1024, 256, 2
KD = D // 128
FW, AW, NH, HD = 256, 768, 12, 64
NK, PH, KH, TOPK = 128, 8, 64, 16
ALPHA = 2.0 ** 0.25
EPS = 1e-5
NQ, QJ = 4, 32
DVE_V = {2: 768, 3: 768, 4: 128, 5: 640}
BODY = 4
C_IOTA, C_BIAS, C_SEQ, C_CHAN, C_INVF, C_IOTA16, C_END = 128, 256, 768, 1792, 2048, 2080, 2304


def peer_encoder(nc, x, c, positions, w_ada, b_ada, w_in, b_in, w_fourier, w_out, b_out, ln1_gain,
                 ln1_bias, w_peer_q, peer_subkeys, peer_u, peer_v, ln2_gain, ln2_bias, table, out):
    f32, i32, u32 = mybir.dt.float32, mybir.dt.int32, mybir.dt.uint32
    f32r, bf16 = mybir.dt.float32r, mybir.dt.bfloat16
    ALU, ACT, AX = mybir.AluOpType, mybir.ActivationFunctionType, mybir.AxisListType
    ds = bass.ds

    x_v = x[0].rearrange("(t p) d -> p t d", p=128)
    out_v = out[0].rearrange("(t p) d -> p t d", p=128)
    pos_v = positions[0].rearrange("(t p) -> p t", p=128)
    ada_v = w_ada[0].rearrange("(k p) n -> p k n", p=128)
    win_v = w_in[0].rearrange("(k p) n -> p k n", p=128)
    wout_v = w_out[0].rearrange("(k p) n -> p k n", p=128)
    wpq_v = w_peer_q[0].rearrange("(k p) n -> p k n", p=128)
    u_v = peer_u[0].rearrange("(i j) d -> i (j d)", i=128)
    v_v = peer_v[0].rearrange("(i j) d -> i (j d)", i=128)
    def piece(view, col):
        return view[:, :, col:col + 512]

    PIECES = [piece(ada_v, n) for n in range(0, 2 * D, 512)]
    PIECES += [piece(win_v, n) for n in range(0, 2560, 512)]
    PIECES += [piece(ada_v, n) for n in (3 * D, 3 * D + 512, 2 * D, 2 * D + 512)]
    PIECES += [piece(wout_v, n) for n in (0, 512)]
    PIECES += [piece(ada_v, n) for n in (4 * D, 4 * D + 512)]
    PIECES += [piece(wpq_v, n) for n in (0, 512)]
    PIECES += [piece(ada_v, n) for n in (5 * D, 5 * D + 512)]
    SH1, SC1, WIN, SH2, GT1, WO, SC2, WPQ, GT2 = 0, 2, 4, 9, 11, 13, 15, 17, 19
    SPLIT = [WIN + n for n in range(5)] + [WO, WO + 1, WPQ, WPQ + 1]
    NSLOT = 5

    with ExitStack() as ctx:
        base = (nc.sbuf_base + 63) // 64 * 64

        def at(name, word, n, dt=f32):
            per = 2 if dt == bf16 else 1
            return nc.alloc_sbuf_tensor_at(name, [128, n * per], dt, offset=base + 4 * word)

        def sem(name):
            return ctx.enter_context(nc.semaphore(name))

        BIG, WORK, CONST, HLO, HSPLIT, XS, UR, G2, SMALL = 0, 24576, 36864, 39168, 41216, 45312, 47360, 51456, 52480
        big = at("big", BIG, 3 * 8192)
        work = at("work", WORK, 12288)
        const = at("const", CONST, C_END)
        hTs = at("hTs", HLO, KD * S)
        rows4 = at("rows4", HSPLIT, 4 * D)
        xs = at("xs", XS, T * D)
        uring = at("uring", UR, 4 * D)
        g2s = at("g2s", G2, D)
        cols = at("cols", SMALL, 58)
        csil = at("csil", SMALL + 64, 8)
        modc = at("modc", SMALL + 72, 32)
        pos_i = at("pos_i", SMALL + 104, T, i32)
        pos_f = at("pos_f", SMALL + 112, T)
        stat = at("stat", SMALL + 120, 2 * 6 + 2 + 2)
        rmax = at("rmax", SMALL + 136, 4 * 4)
        rsum = at("rsum", SMALL + 152, 4 * 4)
        iotab = at("iotab", SMALL + 168, 64, bf16)
        ones = at("ones", SMALL + 232, 128)
        piece_lo = at("piece_lo", BIG, NSLOT * 4096, f32r)
        piece_hi = at("piece_hi", BIG + NSLOT * 4096, 4096, f32r)
        mixh = at("mixh", WORK + 7680, 2048, f32r)
        mixl = at("mixl", HLO, 2048, f32r)
        uth = at("uth", CONST + 256, 2048, f32r)
        utl = at("utl", HLO, 2048, f32r)
        hth = at("hth", HSPLIT, 2048, f32r)
        htl = at("htl", HSPLIT + 2048, 2048, f32r)
        vring = at("vring", WORK, 4096)
        vlo = at("vlo", WORK, 4096, f32r)
        vhi = at("vhi", WORK + 4096, 2048, f32r)
        whi = at("whi", WORK + 7936, 512, f32r)
        wlo = at("wlo", WORK + 8448, 512, f32r)

        ident = const[:, 0:128]
        iota = const[:, C_IOTA:C_IOTA + 128]
        bias_c = const[:, C_BIAS:C_SEQ].rearrange("p (q k) -> p q k", q=2)
        seq_c = const[:, C_SEQ:C_CHAN].rearrange("p (c k t) -> p c k t", c=2, k=2)
        chan_c = const[:, C_CHAN:C_INVF].rearrange("p (c n) -> p c n", c=2)
        invf = const[:, C_INVF:C_IOTA16]
        x3 = xs[:, :].rearrange("p (t d) -> p t d", t=T)
        hT = hTs[:, :].rearrange("p (k t) -> p k t", k=KD)
        slots = [big[:, s * 4096:(s + 1) * 4096].rearrange("p (k n) -> p k n", k=KD) for s in range(NSLOT)]
        bin_row = work[:, 9728:12032]
        g1s, bout_row = rows4[:, 0:D], rows4[:, D:2 * D]
        gain1, bias1 = rows4[:, 2 * D:3 * D], rows4[:, 3 * D:4 * D]
        rope_cs = work[:, 12032:12160].rearrange("p (c t f) -> p c t f", c=2, t=T)
        rope_w = work[:, 12160:12288].rearrange("p (a t f) -> p a t f", a=2, t=T)
        hn = work[:, 0:2048].rearrange("p (t d) -> p t d", t=T)
        qkv = work[:, 0:4608].rearrange("p (t n) -> p t n", t=T)
        qkT = work[:, 4608:7680].rearrange("p (n t) -> p n t", n=12)
        MIXH, MIXL = (x[:, :].rearrange("p (k t) -> p k t", k=KD) for x in (mixh, mixl))
        slots_lo = [piece_lo[:, s * 4096:(s + 1) * 4096].rearrange("p (k n) -> p k n", k=KD) for s in range(NSLOT)]
        HI = piece_hi[:, :].rearrange("p (k n) -> p k n", k=KD)
        rtmp = work[:, 4608:6144].rearrange("p (a n f) -> p a n f", a=2, f=32)
        prob = work[:, 9728:11776].rearrange("p (b q k) -> p b q k", b=4, q=2)
        probT = uring[:, 3072:4096].rearrange("p (b k q) -> p b k q", b=2, k=2)
        fT = uring[:, 0:512].rearrange("p (n t) -> p n t", n=2)
        fw = uring[:, 512:1536].rearrange("p (s n c m) -> p s n c m", s=2, n=2, c=2)
        wfd = uring[:, 1536:1792].rearrange("p (n m) -> p n m", n=2)
        wcs = uring[:, 3072:3584].rearrange("p (n c m) -> p n c m", n=2, c=2)
        rows = uring[0:58, 2304:2432]
        acc1 = work[:, 8704:9728].rearrange("p (a n) -> p a n", a=2)
        acc = work[:, 9728:11776].rearrange("p (a n) -> p a n", a=4)
        acc_s = uring[:, 2048:2560]
        row1, row2 = work[:, 7680:8704], work[:, 10752:11776]
        sub = work[:, 0:4096].rearrange("p (t s h k) -> p t s h k", t=T, s=2, h=PH)
        qpT = work[:, 4096:6144].rearrange("p (h t) -> p h t", h=PH)
        dec = work[:, 4096:6144]
        sk = uring[:, 2048:3072].rearrange("p (h c) -> p h c", h=PH)
        skT = const[:, C_SEQ:C_CHAN].rearrange("p (h k) -> p h k", h=PH)
        cand, candx = (work[:, w:w + 512].rearrange("p (a n) -> p a n", a=2) for w in (6144, 6656))
        subx = work[:, 7168:7424].rearrange("p (a n) -> p a n", a=2)
        sv = work[:, 7424:7680].rearrange("p (h s k) -> p h s k", h=PH, s=2)
        si = work[:, 11792:12048].bitcast(u32).rearrange("p (h s k) -> p h s k", h=PH, s=2)
        sif = work[:, 7680:7936].rearrange("p (h s k) -> p h s k", h=PH, s=2)
        uraw = work[:, 7936:8960].rearrange("p (k i) -> p k i", k=KD)
        OI = work[:, 6144:7168].bitcast(bf16).rearrange("p (b u i) -> p b u i", b=2, u=8)
        OJ = work[:, 7168:7936].bitcast(bf16).rearrange("p (b u c j) -> p b u c j", b=2, u=8, c=3)
        OE = work[:, 9216:9472].bitcast(bf16).rearrange("p (b u j) -> p b u j", b=2, u=8)
        idb = work[:, 9472:9728].bitcast(bf16).rearrange("p (a t) -> p a t", a=2)
        gparts = work[:, 9728:10112].bitcast(bf16).rearrange("p (c t) -> p c t", c=3)
        grest = work[:, 10112:10368]
        tv = work[:, 10368:10624].rearrange("p (t h k) -> p t h k", t=T, h=PH)
        ids = work[:, 10624:11136].rearrange("p (a t n) -> p a t n", a=2, t=T)
        gate = work[:, 11136:11392].rearrange("p (t h k) -> p t h k", t=T, h=PH)
        tpos = work[:, 11392:11520].bitcast(u32)
        posa = work[:, 11520:11648].bitcast(u32)
        posb = work[:, 11648:11776].bitcast(u32)
        gsum = work[:, 11776:11792]
        A4 = [big[:, ((2 + q) % 3) * 8192:((2 + q) % 3 + 1) * 8192] for q in range(NQ)]
        UTH, UTL = (x[:, :].rearrange("p (b k i) -> p b k i", b=2, k=KD) for x in (uth, utl))
        hTH, hTL = (x[:, :].rearrange("p (k t) -> p k t", k=KD) for x in (hth, htl))
        VH = vhi[:, :].rearrange("p (b d) -> p b d", b=2)
        WH, WL = (x[:, :].rearrange("p (b t) -> p b t", b=2) for x in (whi, wlo))
        ys = big[:, 0:2 * D].rearrange("p (t d) -> p t d", t=T)
        gain2, bias2 = uring[:, 0:1024], uring[:, 1024:2048]

        P = [ctx.enter_context(nc.psum_tensor(f"P{i}", [128, 512], f32)) for i in range(8)]
        TR, ACTP, GP, Y = P[0:2], P[2], P[3], P[4:8]

        in_table, in_x, in_rows, in_pos = sem("in_table"), sem("in_x"), sem("in_rows"), sem("in_pos")
        in_table2 = sem("in_table2")
        in_bin, in_bcast, in_wf = sem("in_bin"), sem("in_bcast"), sem("in_wf")
        in_sk, in_ln2 = sem("in_sk"), sem("in_ln2")
        in_piece = [sem(f"in_piece{s}") for s in range(NSLOT)]
        in_u = [sem(f"in_u{s}") for s in range(2)]
        in_v = [sem(f"in_v{s}") for s in range(4)]
        stored = sem("stored")
        pe_rows, cols_ok, csil_ok, ones_ok = sem("pe_rows"), sem("cols_ok"), sem("csil_ok"), sem("ones_ok")
        pe_row, row_ok = sem("pe_row"), sem("row_ok")
        acc_ok, pe_mod, mod_ok = sem("acc_ok"), sem("pe_mod"), sem("mod_ok")
        hn_ok, pe_hT, hT_act, hT_dve = sem("hn_ok"), sem("pe_hT"), sem("hT_act"), sem("hT_dve")
        pe_fT, fT_ok, pe_proj, proj_ok = sem("pe_fT"), sem("fT_ok"), sem("pe_proj"), sem("proj_ok")
        pe_gate, gate1_ok, gate2_ok = sem("pe_gate"), sem("gate1_ok"), sem("gate2_ok")
        split_hi, lo_dve, lo_pool, pe_half = sem("split_hi"), sem("lo_dve"), sem("lo_pool"), sem("pe_half")
        mixl_ok = sem("mixl_ok")
        wf_zero = sem("wf_zero")
        pe_wcs, wcs_ok, pe_fw, fw_ok, pe_mixa = sem("pe_wcs"), sem("wcs_ok"), sem("pe_fw"), sem("fw_ok"), sem("pe_mixa")
        ang_ok, sin_ok, rope_ok = sem("ang_ok"), sem("sin_ok"), sem("rope_ok")
        pe_qkT, qkT_ok, qkT_act = sem("pe_qkT"), sem("qkT_ok"), sem("qkT_act")
        pe_score, smax_ok, exp_ok, norm_ok = sem("pe_score"), sem("smax_ok"), sem("exp_ok"), sem("norm_ok")
        pe_pT, pT_ok, pe_av, mix_ok = sem("pe_pT"), sem("pT_ok"), sem("pe_av"), sem("mix_ok")
        pe_z, ln1_ok, ln1_pool = sem("pe_z"), sem("ln1_ok"), sem("ln1_pool")
        pe_skT, skT_ok, pe_qp, qp_ok, pe_sub, sub_ok = (sem("pe_skT"), sem("skT_ok"), sem("pe_qp"),
                                                        sem("qp_ok"), sem("pe_sub"), sem("sub_ok"))
        topk_ok, gexp_ok, route_ok, pe_idT, idT_ok = (sem("topk_ok"), sem("gexp_ok"),
                                                               sem("route_ok"), sem("pe_idT"), sem("idT_ok"))
        pe_tr0, pe_tr1, uth_ok, utl_ok = sem("pe_tr0"), sem("pe_tr1"), sem("uth_ok"), sem("utl_ok")
        uraw_ok, utl_pool = sem("uraw_ok"), sem("utl_pool")
        hth_ok, htl_ok = sem("hth_ok"), sem("htl_ok")
        pe_act, gelu_ok = sem("pe_act"), sem("gelu_ok")
        equal_ok, onehot_ok, pe_g, gmul_ok = sem("equal_ok"), sem("onehot_ok"), sem("pe_g"), sem("gmul_ok")
        vh_ok, vl_ok, vl_pool = sem("vh_ok"), sem("vl_ok"), sem("vl_pool")
        wh_ok, wl_ok, pe_v = sem("wh_ok"), sem("wl_ok"), sem("pe_v")
        sqrt_ok, var_ok = sem("sqrt_ok"), sem("var_ok")
        dve_chain, topk_chain = sem("dve_chain"), sem("topk_chain")
        alpha_ok, y_out = sem("alpha_ok"), sem("y_out")
        fin_ok, ln2_ok, fin_pool = sem("fin_ok"), sem("ln2_ok"), sem("fin_pool")

        block = ctx.enter_context(nc.Block())

        def when(eng, s, value):
            if not isinstance(value, int) or value > 0:
                eng.wait_ge(s, value)

        def run_quarter(eng, steps, peel_first, peel_last, each=BODY):
            if peel_first:
                for b in range(each):
                    steps(0, b)
            with eng.Fori(int(peel_first), QJ // each - int(peel_last)) as i:
                for b in range(each):
                    steps(i, b)
            if peel_last:
                for b in range(each):
                    steps(QJ // each - 1, b)

        def lower_part(eng, m, half, k0, k1, done):
            slot = SPLIT[m] % NSLOT
            eng.wait_ge(split_hi, 2 * m + half + 1)
            eng.tensor_tensor(slots_lo[slot][:, k0:k1, :], slots[slot][:, k0:k1, :], HI[:, k0:k1, :].bitcast(f32),
                              ALU.subtract).then_inc(done, 1)

        def piece_in(eng, n):
            eng.wait_ge(in_piece[n % NSLOT], 16 * (n // NSLOT + 1))

        @block.sync
        def _(sp):
            sp.dma_start(rows[0:48, :], b_ada[0].rearrange("(a n) -> a n", n=128)).then_inc(in_rows, 16)
            sp.dma_start(rows[48:56, :], c[0].rearrange("(a n) -> a n", n=128)).then_inc(in_rows, 16)
            sp.dma_start(rows[56:58, :], b_in[0, 0:FW].rearrange("(a n) -> a n", n=128)).then_inc(in_rows, 16)
            sp.dma_start(const[:, 0:256], table[:, 0:256]).then_inc(in_table, 16)
            piece_read = [(pe_row, 1), (pe_row, 2), (acc_ok, 1), (acc_ok, 2)] + \
                         [(pe_proj, 2 * n) for n in range(1, 6)] + [(acc_ok, n) for n in range(3, 7)] + \
                         [(pe_z, 2), (pe_z, 4), (pe_row, 3)]
            for n, src in enumerate(PIECES):
                if n >= NSLOT:
                    sp.wait_ge(*piece_read[n - NSLOT])
                sp.dma_start(slots[n % NSLOT], src).then_inc(in_piece[n % NSLOT], 16)
                if n == SH1:
                    sp.dma_start(x3, x_v).then_inc(in_x, 16)
                    sp.dma_start(pos_i[:, :], pos_v, allow_slow_non_contiguous=True).then_inc(in_pos, 16)
                    sp.dma_start(invf, table[:, C_INVF:C_IOTA16]).then_inc(in_pos, 16)
                if n == WIN:
                    sp.dma_start(bin_row, b_in[0, FW:].partition_broadcast(128)).then_inc(in_bin, 16)
                if n == WIN:
                    sp.dma_start(const[:, 256:C_INVF], table[:, 256:C_INVF]).then_inc(in_table2, 16)
                if n == WIN + 2:
                    sp.wait_ge(pe_rows, 1)
                    sp.dma_start(sk, peer_subkeys[0].rearrange("h s k c -> k h s c")).then_inc(in_sk, 16)
                if n == WO + 1:
                    for dst, src in ((g1s, b_ada[0, 2 * D:3 * D]), (bout_row, b_out[0]), (gain1, ln1_gain[0]),
                                     (bias1, ln1_bias[0]), (g2s[:, :], b_ada[0, 5 * D:6 * D])):
                        sp.dma_start(dst, src.partition_broadcast(128)).then_inc(in_bcast, 16)

            def load_u(n, slot):
                sp.dma_start(uring[:, slot * 2048:(slot + 1) * 2048], u_v[:, ds(n * 2048, 2048)])\
                  .then_inc(in_u[slot], 16)

            def load_v(j, slot):
                sp.dma_start(vring[:, slot * D:(slot + 1) * D], v_v[:, ds(j * D, D)]).then_inc(in_v[slot], 16)

            sp.wait_ge(pe_mixa, 1)
            load_u(0, 0)
            sp.wait_ge(pe_av, NH)
            sp.wait_ge(pe_mod, 6)
            load_u(1, 1)
            with sp.Fori(0, 15) as i:
                for b in range(2):
                    sp.wait_ge(pe_tr1, 4 * i + 2 * b + 2)
                    load_u(2 * i + 2 + b, b)
            sp.wait_ge(topk_ok, 1)
            for n in range(4):
                load_v(n, n)

            def next_u(i):
                for b in range(2):
                    sp.wait_ge(pe_tr1, 4 * i + 2 * b + 62)
                    load_u(2 * i + 32 + b, b)
                    if not isinstance(i, int):
                        next_v(i, (2 * b, 2 * b + 1))

            def next_v(i, slots_now):
                for b in slots_now:
                    sp.wait_ge(pe_v, 4 * i + b - 3)
                    load_v(4 * i + b, b)

            next_u(0)
            with sp.Fori(1, 16) as i:
                next_u(i)
            with sp.Fori(16, 32) as i:
                next_v(i, range(4))
            sp.wait_ge(stored, 32)

        @block.gpsimd
        def _(pool):
            pool.memset(wfd, 0.0).then_inc(wf_zero, 1)
            pool.wait_ge(wf_zero, 1)
            for g in range(4):
                h0 = (g % 2) * 64
                pool.dma_start(wfd[h0:h0 + 64, g // 2, h0:h0 + 64], w_fourier[0, g]).then_inc(in_wf, 16)
            for m in range(5):
                for half in range(2):
                    lower_part(pool, m, half, 4 * half, 4 * half + 2, lo_pool)
            for m in range(5, 7):
                for half in range(2):
                    lower_part(pool, m, half, 4 * half, 4 * half + 4, lo_pool)

            pool.wait_ge(ln1_ok, 1)
            pool.wait_ge(in_bcast, 16 * 5)
            pool.tensor_tensor(x3[:, 0, :], x3[:, 0, :], gain1, ALU.mult).then_inc(ln1_pool, 1)
            pool.wait_ge(ln1_pool, 1)
            pool.tensor_tensor(x3[:, 0, :], x3[:, 0, :], bias1, ALU.add).then_inc(ln1_pool, 1)
            for m in range(7, 9):
                for half in range(2):
                    lower_part(pool, m, half, 4 * half, 4 * half + 4, lo_pool)

            def ut_low(b, j):
                for half in range(2):
                    pool.wait_ge(uraw_ok, 2 * j + half + 1)
                    when(pool, pe_act, j - 1)
                    k = slice(4 * half, 4 * half + 4)
                    pool.tensor_tensor(UTL[:, b, k, :], uraw[:, k, :], UTH[:, b, k, :].bitcast(f32),
                                       ALU.subtract).then_inc(utl_pool, 1)

            pool.wait_ge(hth_ok, 4)
            pool.wait_ge(htl_ok, 4)
            ut_low(0, 0)
            for q in range(2):
                run_quarter(pool, lambda i, b: ut_low((b + 1) % 2, i * BODY + b + 1 + QJ * q), q == 0, False)

            for q in range(NQ):
                def steps(i, b):
                    jj = i * BODY + b
                    j = jj + QJ * q
                    pool.wait_ge(wh_ok, j + 1)
                    when(pool, pe_v, j - 1)
                    pool.tensor_tensor(WL[:, b % 2, :], A4[q][:, ds(jj * S, S)], WH[:, b % 2, :].bitcast(f32),
                                       ALU.subtract).then_inc(wl_ok, 1)
                    v0 = DVE_V[q + 2]
                    v = slice(b * D + v0, b * D + D)
                    pool.tensor_tensor(vlo[:, v], vring[:, v], VH[:, b % 2, v0:].bitcast(f32),
                                       ALU.subtract).then_inc(vl_pool, 1)

                run_quarter(pool, steps, q == 0, False)
            pool.wait_ge(y_out, 2)
            pool.wait_ge(alpha_ok, 1)
            pool.wait_ge(gate2_ok, 2)
            pool.tensor_tensor(ys[:, 1, :], ys[:, 1, :], g2s[:, :], ALU.mult).then_inc(fin_pool, 1)
            pool.wait_ge(fin_pool, 1)
            pool.tensor_tensor(x3[:, 1, :], x3[:, 1, :], ys[:, 1, :], ALU.add).then_inc(fin_pool, 1)
            pool.wait_ge(ln2_ok, 1)
            pool.wait_ge(in_ln2, 32)
            pool.tensor_tensor(x3[:, 0, :], x3[:, 0, :], gain2, ALU.mult).then_inc(fin_pool, 1)
            pool.wait_ge(fin_pool, 3)
            pool.tensor_tensor(x3[:, 0, :], x3[:, 0, :], bias2, ALU.add).then_inc(fin_pool, 1)

        @block.scalar
        def _(act):
            act.wait_ge(cols_ok, 1)
            act.activation(csil[:, :], cols[:, 48:56], ACT.Silu).then_inc(csil_ok, 1)

            def root(n):
                act.wait_ge(var_ok, n)
                act.activation(stat[:, 14:15], stat[:, 13:14], ACT.Sqrt).then_inc(sqrt_ok, 1)

            root(1)
            root(2)
            def rows_out(banks, dst, n0):
                for a in range(2):
                    act.wait_ge(pe_row, n0 + a + 1)
                    act.activation(dst[0:1, 512 * a:512 * a + 512], banks[a][0:1, :], ACT.Copy).then_inc(row_ok, 1)

            rows_out((P[6], P[7]), row1, 0)
            def hT_out(m, turn):
                act.wait_ge(mod_ok, 2 * turn)
                for k in range(4):
                    act.wait_ge(pe_hT, 4 * (turn - 1) + k // 2 + 1)
                    act.activation(hT[:, k, :], P[2 + k // 2][:, (k % 2) * S:(k % 2 + 1) * S], ACT.Identity,
                                   bias=modc[:, m + k:m + k + 1], scale=modc[:, m + 8 + k:m + 9 + k])\
                       .then_inc(hT_act, 1)

            PIECE_DONE = [(pe_proj, 2 * n) for n in range(1, 6)] + [(pe_z, 2), (pe_z, 4), (pe_qp, 2)]

            def split_piece(m, halves=(0, 1)):
                piece_in(act, SPLIT[m])
                for half in halves:
                    if m:
                        act.wait_ge(*((pe_half, m), PIECE_DONE[m - 1])[half])
                    k = slice(4 * half, 4 * half + 4)
                    act.activation(HI[:, k, :], slots[SPLIT[m] % NSLOT][:, k, :], ACT.Copy).then_inc(split_hi, 1)

            def h_high(turn):
                for half in range(2):
                    act.wait_ge((hT_act, hT_dve)[half], 4 * turn)
                    k = slice(4 * half, 4 * half + 4)
                    act.activation(hTH[:, k, :], hT[:, k, :], ACT.Copy).then_inc(hth_ok, 1)

            split_piece(0)
            hT_out(0, 1)
            h_high(1)
            split_piece(1, (0,))
            for n in range(2):
                act.wait_ge(pe_fT, n + 1)
                act.activation(fT[:, n, :], P[6 + n][:, 0:S], ACT.Identity, bias=cols[:, 56 + n:57 + n])\
                   .then_inc(fT_ok, 1)
            split_piece(1, (1,))
            act.wait_ge(ang_ok, 1)
            act.activation(rope_cs, rope_w, ACT.Sin).then_inc(sin_ok, 1)
            split_piece(2)
            act.wait_ge(pe_wcs, 1)
            act.activation(wcs, P[0][:, :].rearrange("p (n c m) -> p n c m", n=2, c=2), ACT.Copy).then_inc(wcs_ok, 1)
            split_piece(3)
            for s in range(2):
                act.wait_ge(pe_fw, s + 1)
                act.activation(fw[:, s, :, :, :], P[s][:, :].rearrange("p (n c m) -> p n c m", n=2, c=2),
                               ACT.Copy).then_inc(fw_ok, 1)
            split_piece(4)
            act.wait_ge(pe_mixa, 1)
            act.activation(MIXH[:, 0:2, :], P[6][:, :].rearrange("p (n t) -> p n t", n=2), ACT.Copy).then_inc(mix_ok, 2)
            for n in range(2):
                act.wait_ge(pe_skT, n + 1)
                act.activation(skT[:, 4 * n:4 * n + 4, :], P[n][:, :].rearrange("p (h k) -> p h k", h=4),
                               ACT.Copy).then_inc(skT_ok, 1)
            act.wait_ge(rope_ok, 6)
            for b in (1, 3, 5):
                act.wait_ge(pe_qkT, b + 1)
                act.activation(qkT[:, 2 * b:2 * b + 2, :], P[QK_BANK[b]][:, :].rearrange("p (n t) -> p n t", n=2),
                               ACT.Copy).then_inc(qkT_act, 1)
            def exponentials(h):
                act.wait_ge(smax_ok, h + 1)
                for q in range(2):
                    r = 4 * (h % 4) + q
                    act.activation(prob[:, h % 4, q, :], prob[:, h % 4, q, :], ACT.Exp, bias=rmax[:, r + 2:r + 3],
                                   accum_out=rsum[:, r:r + 1]).then_inc(exp_ok, 1)

            def mixed(pair):
                act.wait_ge(pe_av, 2 * pair + 2)
                act.activation(MIXH[:, 2 + pair, :], P[4 + pair % 2][:, 0:S], ACT.Copy).then_inc(mix_ok, 1)

            exponentials(0)
            for h in range(NH):
                if h + 1 < NH:
                    exponentials(h + 1)
                act.wait_ge(pe_pT, h + 1)
                if h >= 2:
                    act.wait_ge(pe_av, h - 1)
                act.activation(probT[:, h % 2, :, :], P[2 + h % 2][:, :].rearrange("p (k q) -> p k q", k=2),
                               ACT.Copy).then_inc(pT_ok, 1)
                if h >= 2 and h % 2 == 0:
                    mixed(h // 2 - 1)
                if h in (3, 6):
                    split_piece(5, (h // 3 - 1,))
            mixed(NH // 2 - 1)
            split_piece(6)
            for n in range(3, 6):
                root(n)
            rows_out((P[4], P[5]), row2, 2)
            root(6)
            split_piece(7)
            hT_out(16, 2)
            h_high(2)
            split_piece(8)
            for n in range(4):
                act.wait_ge(pe_qp, n + 1)
                act.activation(qpT[:, 2 * n:2 * n + 2, :], P[(6, 7, 0, 1)[n]][:, :].rearrange("p (h t) -> p h t", h=2),
                               ACT.Copy).then_inc(qp_ok, 1)
            for n in range(8):
                t, s, hh = n // 4, n // 2 % 2, n % 2
                act.wait_ge(pe_sub, n + 1)
                act.activation(sub[:, t, s, 4 * hh:4 * hh + 4, :],
                               P[(2, 3, 4, 5, 6, 7, 0, 1)[n]][:, :].rearrange("p (h k) -> p h k", h=4), ACT.Copy)\
                   .then_inc(sub_ok, 1)

            def ut_high(b, j, pool_low=False):
                for half, done in ((0, pe_tr0), (1, pe_tr1)):
                    act.wait_ge(done, j + 1)
                    when(act, pe_act, j - 1)
                    k = slice(4 * half, 4 * half + 4)
                    tr = TR[half][:, :].rearrange("p (k i) -> p k i", k=4)
                    act.activation(UTH[:, b, k, :], tr, ACT.Copy).then_inc(uth_ok, 1)
                    if pool_low:
                        when(act, utl_pool, 2 * j + half - 1)
                        act.activation(uraw[:, k, :], tr, ACT.Copy).then_inc(uraw_ok, 1)

            act.wait_ge(gate2_ok, 2)
            ut_high(0, 0, True)
            for q in range(NQ + 2):
                def steps(i, b):
                    jj = i * BODY + b
                    if q == 0 and isinstance(i, int) and jj == QJ - BODY:
                        act.wait_ge(topk_ok, 1)
                        act.activation(gate, gate, ACT.Exp).then_inc(gexp_ok, 1)
                    if q < NQ and not (isinstance(i, int) and jj + QJ * q == NK - 1):
                        ut_high((b + 1) % 2, jj + 1 + QJ * q, q <= 1)
                    if q >= 2:
                        jv = jj + QJ * (q - 2)
                        act.wait_ge(in_v[b], 16 * (i + QJ // BODY * (q - 2) + 1))
                        when(act, pe_v, jv - 1)
                        act.activation(VH[:, b % 2, :], vring[:, b * D:b * D + D], ACT.Copy).then_inc(vh_ok, 1)
                        act.wait_ge(gmul_ok, QJ * (q - 1))
                        act.activation(WH[:, b % 2, :], A4[q - 2][:, ds(jj * S, S)], ACT.Copy).then_inc(wh_ok, 1)
                    if q < NQ:
                        j = jj + QJ * q
                        act.wait_ge(pe_act, j + 1)
                        if q == 3:
                            act.wait_ge(wl_ok, QJ)
                        act.activation(A4[q][:, ds(jj * S, S)], ACTP[:, 0:S], ACT.Gelu).then_inc(gelu_ok, 1)

                if q == 2:
                    act.wait_ge(utl_pool, 4 * QJ + 2)
                run_quarter(act, steps, q in (0, 2), q in (0, NQ - 1))
            act.wait_ge(pe_tr1, 4 * QJ)
            for dst, src in ((gain2, ln2_gain[0]), (bias2, ln2_bias[0])):
                act.dma_start(dst, src.partition_broadcast(128)).then_inc(in_ln2, 16)
            act.wait_ge(pe_v, 4 * QJ + 1)
            for n in range(2):
                act.activation(ys[:, 1, 512 * n:512 * n + 512], Y[2 + n][:, :], ACT.Copy).then_inc(y_out, 1)
            root(7)
            root(8)
            for t in range(T):
                act.wait_ge(*((fin_pool, 4), (fin_ok, 1))[t])
                act.dma_start(out_v[:, t, :], x3[:, t, :]).then_inc(stored, 16)
            act.wait_ge(stored, 32)

        @block.vector
        def _(dve):
            count = {}

            def link(ins, signal=None):
                s = dve_chain if signal is None else signal
                count[id(s)] = count.get(id(s), 0) + 1
                ins.then_inc(s, 1)
                dve.wait_ge(s, count[id(s)])

            roots = [0]

            def normalise(dst, src, gain=None, bias=None):
                for n in range(2):
                    last = dve.bn_stats(stat[:, 6 * n:6 * n + 6], src[:, 512 * n:512 * n + 512])
                    link(last)
                link(dve.bn_aggr(stat[:, 12:14], stat[:, 0:12].rearrange("p (a b) -> p a b", a=2)))
                roots[0] += 1
                link(dve.tensor_scalar(stat[:, 13:14], stat[:, 13:14], EPS, None, ALU.add), var_ok)
                dve.wait_ge(sqrt_ok, roots[0])
                link(dve.reciprocal(stat[:, 15:16], stat[:, 14:15]))
                if gain is None:
                    return dve.tensor_scalar(dst, src, stat[:, 12:13], stat[:, 15:16], ALU.subtract, ALU.mult)
                link(dve.scalar_tensor_tensor(dst, src, stat[:, 12:13], gain, ALU.subtract, ALU.mult))
                return dve.scalar_tensor_tensor(dst, dst, stat[:, 15:16], bias, ALU.mult, ALU.add)

            def transposed_h(m, turn):
                for k in range(4, 8):
                    dve.wait_ge(pe_hT, 4 * (turn - 1) + k // 2 + 1)
                    dve.tensor_scalar(hT[:, k, :], P[2 + k // 2][:, (k % 2) * S:(k % 2 + 1) * S],
                                      modc[:, m + 8 + k:m + 9 + k], modc[:, m + k:m + k + 1],
                                      ALU.mult, ALU.add).then_inc(hT_dve, 1)

            def weigh(n, acc, ks=range(KD)):
                w = slots[n % NSLOT]
                for k in ks:
                    if k == 0:
                        piece_in(dve, n)
                        link(dve.tensor_scalar(acc, w[:, 0, :], csil[:, 0:1], None, ALU.mult))
                    else:
                        link(dve.scalar_tensor_tensor(acc, w[:, k, :], csil[:, k:k + 1], acc, ALU.mult, ALU.add),
                             acc_ok if k == KD - 1 else None)

            def modulation(chunk, n, one):
                dve.wait_ge(pe_mod, (4, 4, 6, 8)[n])
                m = 8 * n
                link(dve.scalar_tensor_tensor(modc[:, m:m + 8], P[(1, 1, 7, 5)[n]][:, m:m + 8], one,
                                              cols[:, 8 * chunk:8 * chunk + 8], ALU.add, ALU.add), mod_ok)

            def h_low(turn):
                for half in range(2):
                    dve.wait_ge(hth_ok, 2 * turn + half - 1)
                    k = slice(4 * half, 4 * half + 4)
                    dve.tensor_tensor(hTL[:, k, :], hT[:, k, :], hTH[:, k, :].bitcast(f32), ALU.subtract)\
                       .then_inc(htl_ok, 1)

            def lower_half(m, half):
                lower_part(dve, m, half, 4 * half + 2, 4 * half + 4, lo_dve)

            def mixed_low(n, bank):
                dve.wait_ge(mix_ok, n + 1)
                dve.tensor_tensor(MIXL[:, n, :], bank, MIXH[:, n, :].bitcast(f32), ALU.subtract)\
                   .then_inc(mixl_ok, 1)

            def gate_out(g, banks, n, done):
                for a in range(2):
                    dve.wait_ge(pe_gate, n + a + 1)
                    s = slice(512 * a, 512 * a + 512)
                    dve.scalar_tensor_tensor(g[:, s], banks[a][:, :], 1.0, g[:, s], ALU.add, ALU.add).then_inc(done, 1)

            dve.memset(ones[:, :], 1.0).then_inc(ones_ok, 1)
            dve.wait_ge(pe_rows, 1)
            link(dve.tensor_copy(cols[:, :], P[0][:, 0:58]), cols_ok)
            dve.wait_ge(in_x, 16)
            for t in range(T):
                link(normalise(hn[:, t, :], x3[:, t, :]), hn_ok)
            dve.wait_ge(in_pos, 32)
            link(dve.tensor_copy(pos_f[:, :], pos_i[:, :]))
            for t in range(T):
                for a in range(2):
                    link(dve.tensor_scalar(rope_w[:, a, t, :], invf, pos_f[:, t:t + 1], None, ALU.mult))
            TURN = 2.0 * math.pi
            C1 = 6.28125
            C2 = float(np.float32(np.round((TURN - C1) * 2 ** 21) / 2 ** 21))
            C3 = float(np.float32(TURN - C1 - C2))
            ROUND = 12582912.0
            for a, lead in ((0, 0.25), (1, 0.0)):
                w, n = rope_w[:, a, :, :], rope_cs[:, a, :, :]
                link(dve.tensor_scalar(n, w, 1.0 / TURN, lead, ALU.mult, ALU.add))
                link(dve.tensor_scalar(n, n, ROUND, None, ALU.add))
                link(dve.tensor_scalar(n, n, ROUND, None, ALU.subtract))
                for part in (C1, C2, C3):
                    link(dve.scalar_tensor_tensor(w, n, -part, w, ALU.mult, ALU.add))
                if a == 0:
                    link(dve.tensor_scalar(w, w, math.pi / 2, None, ALU.add))
                lim = 3.1415925
                link(dve.tensor_scalar(w, w, -lim, lim, ALU.max, ALU.min))
            link(dve.tensor_copy(pos_f[:, :], pos_i[:, :]), ang_ok)
            dve.wait_ge(csil_ok, 1)
            for n in range(2):
                weigh(SC1 + n, acc1[:, n, :])
            lower_half(0, 0)
            modulation(0, 0, 0.0)
            modulation(1, 1, 1.0)
            transposed_h(0, 1)
            h_low(1)
            for m, half in ((0, 1), (1, 0), (1, 1)):
                lower_half(m, half)

            def rotate(n0, n1, t):
                n = n1 - n0
                qk = qkv[:, t, n0 * HD:n1 * HD].rearrange("p (n two f) -> p n two f", two=2, f=32)
                cs = rope_cs[:, 0, t, :].unsqueeze(1).to_broadcast([128, n, 32])
                sn = rope_cs[:, 1, t, :].unsqueeze(1).to_broadcast([128, n, 32])
                t1, t2 = qk[:, :, 0, :], qk[:, :, 1, :]
                link(dve.tensor_tensor(rtmp[:, 0, 0:n], t1, sn, ALU.mult))
                link(dve.tensor_tensor(rtmp[:, 1, 0:n], t2, sn, ALU.mult))
                link(dve.tensor_tensor(t1, t1, cs, ALU.mult))
                link(dve.tensor_tensor(t2, t2, cs, ALU.mult))
                link(dve.tensor_tensor(t1, t1, rtmp[:, 1, 0:n], ALU.subtract))
                link(dve.tensor_tensor(t2, t2, rtmp[:, 0, 0:n], ALU.add), rope_ok)

            dve.wait_ge(in_bin, 16)
            dve.wait_ge(pe_hT, 4)
            HEADS = ((), (0, 12), (12, 20), (20, 24), ())
            for m in range(5):
                for g in (2 * m, 2 * m + 1):
                    t, c0, n = GROUPS[g]
                    dve.wait_ge(pe_proj, g + 1)
                    dve.tensor_tensor(qkv[:, t, c0:c0 + n], P[2 + g % 4][:, 0:n], bin_row[:, c0:c0 + n], ALU.add)\
                       .then_inc(proj_ok, 1)
                if m == 1:
                    dve.wait_ge(sin_ok, 1)
                for t in range(T):
                    if m + 2 < 5:
                        lower_half(m + 2, t)
                    if HEADS[m]:
                        dve.wait_ge(proj_ok, 2 * m + 2)
                        rotate(*HEADS[m], t)
                    if (m, t) == (0, 1):
                        weigh(SH2, acc1[:, 0, :])
            for b in (0, 2, 4):
                dve.wait_ge(pe_qkT, b + 1)
                dve.tensor_copy(qkT[:, 2 * b:2 * b + 2, :], P[QK_BANK[b]][:, :].rearrange("p (n t) -> p n t", n=2))\
                   .then_inc(qkT_ok, 1)
            dve.wait_ge(mix_ok, 2)
            dve.tensor_tensor(MIXL[:, 0:2, :], P[6][:, :].rearrange("p (n t) -> p n t", n=2),
                              MIXH[:, 0:2, :].bitcast(f32), ALU.subtract).then_inc(mixl_ok, 2)
            dve.wait_ge(in_table2, 16)
            def score_max(h):
                dve.wait_ge(pe_score, h + 1)
                if h >= 4:
                    dve.wait_ge(pe_pT, h - 3)
                r = rmax[:, 4 * (h % 4):4 * (h % 4) + 4]
                for q in range(2):
                    link(dve.tensor_tensor_reduce(out=prob[:, h % 4, q, :], in0=P[h % 2][:, q * S:(q + 1) * S],
                                                  in1=bias_c[:, q, :], scale=HD ** -0.5, scalar=-3.0e38,
                                                  op0=ALU.add, op1=ALU.max, accum_out=r[:, q:q + 1]))
                link(dve.tensor_scalar(r[:, 2:4], r[:, 0:2], -1.0, None, ALU.mult), smax_ok)

            def over_sum(h):
                dve.wait_ge(exp_ok, 2 * h + 2)
                r = rsum[:, 4 * (h % 4):4 * (h % 4) + 4]
                link(dve.reciprocal(r[:, 2:4], r[:, 0:2]))
                for q in range(2):
                    dve.tensor_scalar(prob[:, h % 4, q, :], prob[:, h % 4, q, :], r[:, 2 + q:3 + q], None,
                                      ALU.mult).then_inc(norm_ok, 1)

            dve.wait_ge(pe_skT, 2)
            score_max(0)
            score_max(1)
            for h in range(NH):
                over_sum(h)
                if h + 2 < NH:
                    score_max(h + 2)
                if h < KD:
                    weigh(SH2 + 1, acc_s, (h,))
                if h >= 3 and h % 2:
                    mixed_low(2 + (h - 3) // 2, P[4 + (h - 3) // 2 % 2][:, 0:S])
            mixed_low(2 + 5, P[5][:, 0:S])
            dve.wait_ge(pe_pT, NH)
            for n in range(2):
                weigh(GT1 + n, acc[:, n, :])
            modulation(3, 2, 0.0)
            dve.wait_ge(in_bcast, 16 * 5)
            gate_out(g1s, (P[2], P[3]), 0, gate1_ok)
            dve.wait_ge(gate1_ok, 2)
            link(dve.tensor_tensor(bout_row, bout_row, g1s, ALU.mult))
            for t in range(T):
                link(dve.scalar_tensor_tensor(x3[:, t, :], x3[:, t, :], ALPHA, bout_row, ALU.mult, ALU.add))
            for t in range(T):
                for n in range(2):
                    s = slice(512 * n, 512 * n + 512)
                    dve.wait_ge(pe_z, 2 * n + t + 1)
                    link(dve.tensor_tensor(hn[:, t, s], P[(6, 7, 0, 1)[2 * t + n]][:, :], g1s[:, s], ALU.mult))
                link(dve.tensor_tensor(x3[:, t, :], x3[:, t, :], hn[:, t, :], ALU.add))
                if t == 0:
                    link(normalise(x3[:, t, :], x3[:, t, :]), ln1_ok)
                else:
                    link(normalise(x3[:, t, :], x3[:, t, :], gain1, bias1))
            dve.wait_ge(ln1_pool, 2)
            link(normalise(hn[:, 0, :], x3[:, 0, :]), hn_ok)
            link(normalise(hn[:, 1, :], x3[:, 1, :]), hn_ok)
            modulation(4, 3, 1.0)
            transposed_h(16, 2)
            h_low(2)
            for n in range(2):
                weigh(GT2 + n, acc[:, 2 + n, :])
            gate_out(g2s, (P[2], P[3]), 2, gate2_ok)

            def ut_low(b, j):
                for half in range(2):
                    dve.wait_ge(uth_ok, 2 * j + half + 1)
                    when(dve, pe_act, j - 1)
                    k = slice(4 * half, 4 * half + 4)
                    dve.tensor_tensor(UTL[:, b, k, :], TR[half][:, :].rearrange("p (k i) -> p k i", k=4),
                                      UTH[:, b, k, :].bitcast(f32), ALU.subtract).then_inc(utl_ok, 1)

            done = [0]

            def signal(ins):
                done[0] += 1
                ins.then_inc(topk_chain, 1)
                return done[0]

            def top16(lists):
                def each(op, after):
                    out = []
                    for a, one in enumerate(lists):
                        if after:
                            dve.wait_ge(topk_chain, after[a])
                        out.append(signal(op(*one)))
                    return out

                n = each(lambda v, x, best, at: dve.max(best[:, 0:8], v), None)
                each(lambda v, x, best, at: dve.max_index(at[:, 0:8], best[:, 0:8], v), n)
                n = each(lambda v, x, best, at: dve.match_replace(x, best[:, 0:8], v, -3.0e38), None)
                n = each(lambda v, x, best, at: dve.max(best[:, 8:16], x), n)
                n = each(lambda v, x, best, at: dve.max_index(at[:, 8:16], best[:, 8:16], x), n)
                return n

            def head_keys(t, h):
                n = top16([(sub[:, t, s, h, :], subx[:, s, :], sv[:, h, s, :], si[:, h, s, :]) for s in range(2)])
                dve.wait_ge(topk_chain, n[-1])

            def head_pairs(t, h):
                for a in range(2):
                    n = signal(dve.tensor_tensor(
                        cand[:, a, :].rearrange("p (a b) -> p a b", a=TOPK),
                        sv[:, h + a, 0, :].unsqueeze(2).to_broadcast([128, TOPK, TOPK]),
                        sv[:, h + a, 1, :].unsqueeze(1).to_broadcast([128, TOPK, TOPK]), ALU.add))
                dve.wait_ge(topk_chain, n)
                n = top16([(cand[:, a, :], candx[:, a, :], tv[:, t, h + a, :],
                            tpos[:, (h + a) * TOPK:(h + a + 1) * TOPK]) for a in range(2)])
                dve.wait_ge(topk_chain, n[-1])

            def key_ids(t):
                link(dve.tensor_copy(sif, si))
                link(dve.tensor_scalar(posa, tpos, 4, None, ALU.logical_shift_right))
                link(dve.tensor_scalar(posb, tpos, 15, None, ALU.bitwise_and))
                i16 = iota[:, 0:16].unsqueeze(1).to_broadcast([128, 128, 16])
                d3 = dec.rearrange("p (n a) -> p n a", a=16)
                d4 = dec.rearrange("p (h k a) -> p h k a", h=PH, k=TOPK)
                for s, where in ((0, posa), (1, posb)):
                    link(dve.tensor_tensor(d3, where.unsqueeze(2).to_broadcast([128, 128, 16]), i16, ALU.is_equal))
                    link(dve.tensor_tensor(d4, d4, sif[:, :, s, :].unsqueeze(2).to_broadcast([128, PH, TOPK, 16]),
                                           ALU.mult))
                    link(dve.tensor_reduce(ids[:, s, t, :], d3, AX.X, ALU.add))

            for t in range(T):
                dve.wait_ge(sub_ok, 4 * t + 4)
                for h in range(0, PH, 2):
                    head_keys(t, h)
                    head_keys(t, h + 1)
                    head_pairs(t, h)
                if t == T - 1:
                    link(dve.tensor_tensor(gate, tv, tv[:, :, :, 0:1].to_broadcast([128, T, PH, TOPK]),
                                           ALU.subtract), topk_ok)
                dve.wait_ge(sub_ok, 8)
                key_ids(t)
            link(dve.tensor_copy(iotab[:, :], iota))
            dve.wait_ge(gexp_ok, 1)
            g2 = gsum.rearrange("p (t h) -> p t h", t=T)
            link(dve.tensor_reduce(g2, gate, AX.X, ALU.add))
            link(dve.reciprocal(gsum, gsum))
            link(dve.tensor_tensor(gate, gate, g2.unsqueeze(3).to_broadcast([128, T, PH, TOPK]), ALU.mult), route_ok)
            for t, bank in ((0, GP), (1, Y[0])):
                dve.wait_ge(pe_idT, t + 1)
                tok = slice(128 * t, 128 * t + 128)
                link(dve.tensor_copy(idb[:, :, tok], bank[:, 0:256].rearrange("p (a t) -> p a t", a=2)))
                link(dve.tensor_copy(grest[:, tok], bank[:, 256:384]), idT_ok)
            for n in range(3):
                link(dve.tensor_copy(gparts[:, n, :], grest))
                if n < 2:
                    link(dve.tensor_tensor(grest, grest, gparts[:, n, :], ALU.subtract))

            def onehots(q, g, b, n):
                by_i = idb[:, 0, ds(g * 8, 8)].unsqueeze(2).to_broadcast([128, 8, 128])
                by_j = idb[:, 1, ds(g * 8, 8)].unsqueeze(2).to_broadcast([128, 8, QJ])
                dve.tensor_tensor(OE[:, b], iotab[:, QJ * q:QJ * q + QJ].unsqueeze(1).to_broadcast([128, 8, QJ]),
                                  by_j, ALU.is_equal).then_inc(equal_ok, 1)
                dve.tensor_tensor(OI[:, b], iotab[:, :].unsqueeze(1).to_broadcast([128, 8, 128]), by_i, ALU.is_equal)
                dve.wait_ge(equal_ok, n + 1)
                dve.tensor_tensor(OJ[:, b], OE[:, b].unsqueeze(2).to_broadcast([128, 8, 3, QJ]),
                                  gparts[:, :, ds(g * 8, 8)].rearrange("p c u -> p u c").unsqueeze(3)
                                  .to_broadcast([128, 8, 3, QJ]), ALU.mult).then_inc(onehot_ok, 1)

            def apply_gates(q, g, n):
                dve.wait_ge(pe_g, n + 1)
                dve.wait_ge(gelu_ok, QJ * (q + 1))
                a = A4[q].rearrange("p (j t) -> p j t", t=S)[:, :, ds(g * 8, 8)]
                dve.tensor_tensor(a, a, GP[:, 0:256].rearrange("p (u j) -> p j u", u=8), ALU.mult)\
                   .then_inc(gmul_ok, 1)

            onehots(0, 0, 0, 0)
            for q in range(1, NQ + 2):
                def steps(i, b):
                    jj = i * BODY + b
                    end = isinstance(i, int) and jj == QJ - 1
                    if 2 <= q < NQ and not (end and q == NQ - 1):
                        ut_low((b + 1) % 2, jj + 1 + QJ * q)
                    if q >= 2:
                        dve.wait_ge(vh_ok, jj + QJ * (q - 2) + 1)
                        v = slice(b * D, b * D + DVE_V[q])
                        dve.tensor_tensor(vlo[:, v], vring[:, v], VH[:, b % 2, 0:DVE_V[q]].bitcast(f32), ALU.subtract)\
                           .then_inc(vl_ok, 1)
                    if q <= NQ and not end:
                        onehots(q - 1, jj + 1, (b + 1) % 2, jj + 1 + QJ * (q - 1))
                    elif q < NQ:
                        onehots(q, 0, 0, QJ * q)
                    if q <= NQ:
                        apply_gates(q - 1, jj, jj + QJ * (q - 1))

                run_quarter(dve, steps, False, q <= NQ)
            link(dve.tensor_scalar(x3[:, 1, :], x3[:, 1, :], ALPHA, None, ALU.mult), alpha_ok)
            dve.wait_ge(in_ln2, 32)
            dve.wait_ge(pe_v, 4 * QJ)
            for n in range(2):
                s = slice(512 * n, 512 * n + 512)
                link(dve.tensor_tensor(ys[:, 0, s], Y[n][:, :], g2s[:, s], ALU.mult))
            link(dve.scalar_tensor_tensor(x3[:, 0, :], x3[:, 0, :], ALPHA, ys[:, 0, :], ALU.mult, ALU.add))
            link(normalise(x3[:, 0, :], x3[:, 0, :]), ln2_ok)
            dve.wait_ge(fin_pool, 2)
            link(normalise(x3[:, 1, :], x3[:, 1, :], gain2, bias2), fin_ok)

        @block.tensor
        def _(pe):
            mm = pe.matmul

            def transpose(dst, src):
                return pe.transpose(dst, src, ident[0:src.shape[0], 0:src.shape[0]])

            def three_passes(m, units, h_parts=None):
                for half in range(2):
                    if h_parts is not None:
                        pe.wait_ge(hth_ok, h_parts + half + 1)
                        pe.wait_ge(htl_ok, h_parts + half + 1)
                    pe.wait_ge(split_hi, 2 * m + half + 1)
                    pe.wait_ge(lo_pool, 2 * m + half + 1)
                    if m < 5:
                        pe.wait_ge(lo_dve, 2 * m + half + 1)
                    for n, (out_ap, operands, opens, signal) in enumerate(units):
                        for k in range(4 * half, 4 * half + 4):
                            for i, (a, b) in enumerate(operands(k)):
                                last = mm(out_ap, a, b, start=(opens and k == 0 and i == 0),
                                          stop=(k == KD - 1 and i == 2), skip_group_check=m >= 7)
                        if half == 0 and n == len(units) - 1:
                            last.then_inc(pe_half, 1)
                        if half == 1 and signal is not None:
                            last.then_inc(signal, 1)

            def weights_moving(m, hi, lo, t, c0, n):
                w = slots_lo[SPLIT[m] % NSLOT]
                tok, col = slice(t * 128, t * 128 + 128), slice(c0, c0 + n)
                return lambda k: ((hi[:, k, tok], HI[:, k, col]), (lo[:, k, tok], HI[:, k, col]),
                                  (hi[:, k, tok], w[:, k, col]))

            def weights_still(m, hi, lo, c0):
                w, col = slots_lo[SPLIT[m] % NSLOT], slice(c0, c0 + 128)
                return lambda k: ((HI[:, k, col], hi[:, k, :]), (HI[:, k, col], lo[:, k, :]),
                                  (w[:, k, col], hi[:, k, :]))

            def mod_row(n, bank):
                piece_in(pe, n)
                for k in range(KD):
                    last = mm(bank[0:1, :], csil[:, k:k + 1], slots[n % NSLOT][:, k, :],
                              start=(k == 0), stop=(k == KD - 1))
                last.then_inc(pe_row, 1)

            def row_columns(src, ready, m, bank):
                pe.wait_ge(row_ok, ready)
                for a in range(8):
                    last = mm(bank[:, m + a:m + a + 1], src[0:1, a * 128:a * 128 + 128], ones[0:1, 0:1],
                              start=True, stop=True)
                last.then_inc(pe_mod, 2)

            def acc_columns(src, ready, m, bank):
                pe.wait_ge(acc_ok, ready)
                for a in range(4):
                    last = mm(bank[:, m + a:m + a + 1], src[:, a * 128:a * 128 + 128], ones[:, 0:1],
                              start=True, stop=True)
                last.then_inc(pe_mod, 1)

            def gate_rows(acc, n, banks):
                pe.wait_ge(acc_ok, n)
                for a in range(2):
                    mm(banks[a][:, :], ones[:, :], acc[:, a, :], start=True, stop=True).then_inc(pe_gate, 1)

            def h_transposes(turn, mod_bank=None):
                pe.wait_ge(hn_ok, 2 * turn)
                for b in range(4):
                    if b == mod_bank:
                        pe.wait_ge(mod_ok, 4)
                    for kk in range(2):
                        for t in range(T):
                            k = 2 * b + kk
                            last = transpose(P[2 + b][:, kk * S + t * 128:kk * S + t * 128 + 128],
                                             hn[:, t, k * 128:k * 128 + 128])
                    last.then_inc(pe_hT, 1)

            pe.wait_ge(in_table, 16)
            pe.wait_ge(in_rows, 48)
            transpose(P[0][:, 0:58], rows).then_inc(pe_rows, 1)
            pe.wait_ge(csil_ok, 1)
            for n in range(2):
                mod_row(SH1 + n, P[6 + n])
            h_transposes(1)
            pe.wait_ge(ones_ok, 1)
            row_columns(row1, 2, 0, P[1])
            for n in range(2):
                acc_columns(acc1[:, n, :], 1 + n, 8 + 4 * n, P[1])
            def fourier_weights():
                pe.wait_ge(in_wf, 64)
                pe.wait_ge(in_table2, 16)
                pe.wait_ge(cols_ok, 1)
                for n in range(2):
                    for cs in range(2):
                        last = mm(P[0][:, n * 256 + cs * 128:n * 256 + cs * 128 + 128], chan_c[:, cs, :],
                                  wfd[:, n, :], start=True, stop=True)
                last.then_inc(pe_wcs, 1)

            def fourier_channels():
                pe.wait_ge(wcs_ok, 1)
                pe.wait_ge(fT_ok, 2)
                pe.wait_ge(mod_ok, 2)
                for s in range(2):
                    for n in range(2):
                        last = mm(P[s][:, n * 256:n * 256 + 256], fT[:, n, s * 128:s * 128 + 128],
                                  wcs[:, n, :, :].rearrange("p c m -> p (c m)"), start=True, stop=True)
                    last.then_inc(pe_fw, 1)

            def fourier_positions():
                pe.wait_ge(fw_ok, 2)
                for n in range(2):
                    for i, (cs, s) in enumerate(((0, 0), (0, 1), (1, 0), (1, 1))):
                        last = mm(P[6][:, n * S:n * S + S], fw[:, s, n, cs, :], seq_c[:, cs, s, :],
                                  start=(i == 0), stop=(i == 3))
                last.then_inc(pe_mixa, 1)
                acc_columns(acc1[:, 0, :], 3, 16, P[7])

            def subkeys():
                pe.wait_ge(in_sk, 16)
                for n in range(2):
                    for h in range(4):
                        last = transpose(P[n][:, h * 128:h * 128 + 128], sk[:, 4 * n + h, :])
                    last.then_inc(pe_skT, 1)

            BETWEEN = {1: fourier_weights, 2: fourier_channels, 3: fourier_positions, 4: subkeys}
            for m in range(5):
                units = []
                if m == 0:
                    units = [(P[6 + n][:, 0:S], weights_still(0, hTH, hTL, n * 128), True, pe_fT) for n in range(2)]
                for g in (2 * m, 2 * m + 1):
                    t, c0, n = GROUPS[g]
                    units.append((P[2 + g % 4][:, 0:n], weights_moving(m, hTH, hTL, t, FW if m == 0 else 0, n),
                                  True, pe_proj))
                if m >= 2:
                    pe.wait_ge(proj_ok, 2 * m - 2)
                three_passes(m, units, 0 if m == 0 else None)
                if m in BETWEEN:
                    BETWEEN[m]()
            for b in range(6):
                if b == 0:
                    pe.wait_ge(rope_ok, 2)
                    pe.wait_ge(proj_ok, 8)
                if b == 2:
                    pe.wait_ge(proj_ok, 10)
                if b == 3:
                    pe.wait_ge(rope_ok, 6)
                if b >= 4:
                    pe.wait_ge((qkT_ok, qkT_act)[b - 4], 1)
                for kk in range(2):
                    for t in range(T):
                        n = 2 * b + kk
                        last = transpose(P[QK_BANK[b]][:, kk * S + t * 128:kk * S + t * 128 + 128],
                                         qkv[:, t, n * 128:n * 128 + 128])
                last.then_inc(pe_qkT, 1)

            def scores(h):
                p0 = (h % 2) * 64
                if h >= 2:
                    pe.wait_ge(smax_ok, h - 1)
                for q in range(2):
                    last = mm(P[h % 2][:, q * S:(q + 1) * S], qkT[p0:p0 + 64, h // 2, q * 128:q * 128 + 128],
                              qkT[p0:p0 + 64, 6 + h // 2, :], start=True, stop=True)
                last.then_inc(pe_score, 1)

            def attend(h):
                pe.wait_ge(norm_ok, 2 * h + 2)
                if h >= 2:
                    pe.wait_ge(pT_ok, h - 1)
                for k in range(2):
                    for q in range(2):
                        last = transpose(P[2 + h % 2][:, k * S + q * 128:k * S + q * 128 + 128],
                                         prob[:, h % 4, q, k * 128:k * 128 + 128])
                last.then_inc(pe_pT, 1)

            def values(h):
                p0 = (h % 2) * 64
                pe.wait_ge(pT_ok, h + 1)
                if h >= 4:
                    pe.wait_ge(mixl_ok, 2 + h // 2 - 1)
                for k in range(2):
                    last = mm(P[4 + (h // 2) % 2][p0:p0 + 64, 0:S], qkv[:, k, 2 * AW + h * HD:2 * AW + h * HD + HD],
                              probT[:, h % 2, k, :], start=(k == 0), stop=(k == 1))
                last.then_inc(pe_av, 1)

            pe.wait_ge(qkT_ok, 3)
            pe.wait_ge(qkT_act, 3)
            pe.wait_ge(skT_ok, 2)
            scores(0)
            scores(1)
            for h in range(NH + 1):
                if h + 2 < NH:
                    scores(h + 2)
                if h < NH:
                    attend(h)
                if h >= 1:
                    values(h - 1)
                if h == 10:
                    acc_columns(acc_s, 4, 20, P[7])
            pe.wait_ge(mix_ok, 8)
            pe.wait_ge(mixl_ok, 8)
            pe.wait_ge(smax_ok, NH)
            for n in range(2):
                if n == 1:
                    pe.wait_ge(pT_ok, NH)
                    gate_rows(acc[:, 0:2, :], 6, (P[2], P[3]))
                    pe.wait_ge(mod_ok, 3)
                three_passes(5 + n, [(P[(6, 7, 0, 1)[2 * t + n]][:, :],
                                      weights_moving(5 + n, MIXH, MIXL, t, 0, 512), True, pe_z) for t in range(T)])
            for n in range(2):
                mod_row(SC2 + n, P[4 + n])
            row_columns(row2, 4, 24, P[5])
            h_transposes(2, 3)
            for m in (7, 8):
                units = []
                for h in range(4 * (m - 7), 4 * (m - 7) + 4):
                    bank = (6, 7, 0, 1)[h // 2]
                    units.append((P[bank][:, h % 2 * S:h % 2 * S + S], weights_still(m, hTH, hTL, h % 4 * 128),
                                  h % 2 == 0, pe_qp if h % 2 else None))
                three_passes(m, units, 2 if m == 7 else None)
            for a in range(2):
                pe.wait_ge(acc_ok, 7 + a)
                mm(P[2 + a][:, :], ones[:, :], acc[:, 2 + a, :], start=True, stop=True).then_inc(pe_gate, 1)
            pe.wait_ge(qp_ok, 4)
            pe.wait_ge(gate2_ok, 2)
            for n in range(8):
                t, s, hh = n // 4, n // 2 % 2, n % 2
                for h in range(4 * hh, 4 * hh + 4):
                    last = mm(P[(2, 3, 4, 5, 6, 7, 0, 1)[n]][:, (h % 4) * 128:(h % 4) * 128 + 128],
                              qpT[64 * s:64 * s + 64, h, t * 128:t * 128 + 128], skT[64 * s:64 * s + 64, h, :],
                              start=True, stop=True)
                last.then_inc(pe_sub, 1)
            pe.wait_ge(sub_ok, 8)

            def u_transposes(slot, j, turn, by_act=True):
                if slot % 2 == 0:
                    pe.wait_ge(in_u[slot // 2], turn)
                for half, done in ((0, pe_tr0), (1, pe_tr1)):
                    if by_act:
                        when(pe, uraw_ok, 2 * j + half - 1)
                    else:
                        pe.wait_ge(utl_ok, 2 * (j - 2 * QJ - 1) + half - 1)
                    for k in range(4):
                        kk = 4 * half + k
                        last = transpose(TR[half][:, k * 128:k * 128 + 128],
                                         uring[:, slot * D + kk * 128:slot * D + kk * 128 + 128])
                    last.then_inc(done, 1)

            def u_product(b, j, by_pool):
                pe.wait_ge(uth_ok, 2 * j + 2)
                when(pe, gelu_ok, j)
                for k in range(KD):
                    mm(ACTP[:, 0:S], UTH[:, b, k, :], hTH[:, k, :], start=(k == 0), stop=False)
                    mm(ACTP[:, 0:S], UTH[:, b, k, :], hTL[:, k, :], start=False, stop=False)
                pe.wait_ge(utl_pool if by_pool else utl_ok, 2 * j + 2 - (0 if by_pool else 4 * QJ + 2))
                for k in range(KD):
                    last = mm(ACTP[:, 0:S], UTL[:, b, k, :], hTH[:, k, :], start=False, stop=(k == KD - 1))
                last.then_inc(pe_act, 1)

            def gates(b, n):
                pe.wait_ge(onehot_ok, n + 1)
                when(pe, gmul_ok, n)
                for u in range(8):
                    for part in range(3):
                        last = mm(GP[:, u * QJ:u * QJ + QJ], OI[:, b, u, :], OJ[:, b, u, part, :],
                                  start=(part == 0), stop=(part == 2))
                last.then_inc(pe_g, 1)

            def v_product(slot, j, first=False, final=False):
                pe.wait_ge(wh_ok, j + 1)
                b = slot % 2

                def one(w, v, v0, start, stop, tiles=range(T)):
                    for t in tiles:
                        for n in range(2):
                            last = mm(Y[2 * t + n][:, :], w[:, b, t * 128:t * 128 + 128],
                                      v[:, v0 + 512 * n:v0 + 512 * n + 512], start=start, stop=stop)
                    return last

                one(WH, vhi, b * D, first, False)
                pe.wait_ge(wl_ok, j + 1)
                if not final:
                    one(WL, vhi, b * D, False, False)
                pe.wait_ge(vl_ok, j + 1)
                pe.wait_ge(vl_pool, j + 1)
                if final:
                    for t in range(T):
                        one(WL, vhi, b * D, False, False, (t,))
                        one(WH, vlo, slot * D, False, True, (t,)).then_inc(pe_v, 1)
                    return
                one(WH, vlo, slot * D, False, False).then_inc(pe_v, 1)

            def route_transposes():
                pe.wait_ge(route_ok, 1)
                for t, bank in ((0, GP), (1, Y[0])):
                    for a in range(3):
                        src = ids[:, a, t, :] if a < 2 else gate[:, t, :, :].rearrange("p h k -> p (h k)")
                        last = transpose(bank[:, a * 128:a * 128 + 128], src)
                    last.then_inc(pe_idT, 1)

            u_transposes(0, 0, 16)
            for q in range(NQ + 2):
                u_on, g_on, v_on = q < NQ, 1 <= q < NQ + 1, q >= 2

                def steps(i, b):
                    jj = i * BODY + b
                    if q == 0 and isinstance(i, int) and jj == QJ - 1:
                        route_transposes()
                    if u_on and not (q == NQ - 1 and isinstance(i, int) and jj == QJ - 1):
                        u_transposes((b + 1) % BODY, jj + 1 + QJ * q, 16 * (i + QJ // BODY * q + 1 + (b == BODY - 1)),
                                     q < 2 or (q == 2 and isinstance(i, int) and jj == 0))
                    if u_on:
                        u_product(b % 2, jj + QJ * q, q < 2 or (q == 2 and isinstance(i, int) and jj == 0))
                    if g_on:
                        gates(b % 2, jj + QJ * (q - 1))
                    if v_on:
                        v_product(b, jj + QJ * (q - 2), first=q == 2 and isinstance(i, int) and jj == 0,
                                  final=q == NQ + 1 and isinstance(i, int) and jj == QJ - 1)

                head = q <= 2
                tail = q in (0, NQ - 1, NQ + 1)
                run_quarter(pe, steps, head, tail)


QK_BANK = (4, 5, 2, 3, 4, 5)
GROUPS = [(t, 0, 256) for t in range(2)] + [(t, c, 512) for c in range(256, 2304, 512) for t in range(2)]


def constant_table():
    tab = np.zeros((128, C_END), np.float64)
    p = np.arange(128)
    tab[:, 0:128] = np.eye(128)
    tab[:, C_IOTA:C_IOTA + 128] = np.arange(128)
    q = p[:, None, None] + 128 * np.arange(2)[None, :, None]
    off = np.arange(S)[None, None, :] - q
    n = np.zeros(off.shape)
    for window, dil in ((128, 1), (512, 4), (2048, 16)):
        n += (off % dil == 0) & (np.abs(off) <= window // 2)
    tab[:, C_BIAS:C_SEQ] = (np.where(n > 0, np.log(np.maximum(n, 1)), -1e30) * HD ** 0.5).reshape(128, -1)
    s = p[:, None, None] + 128 * np.arange(2)[None, :, None]
    ang = 2 * np.pi * ((s * np.arange(S)[None, None, :]) % S) / S
    norm = 1.0 / math.sqrt(S * 64)
    tab[:, C_SEQ:C_CHAN] = np.stack([np.cos(ang) * norm, -np.sin(ang) * norm], 1).reshape(128, -1)
    c = np.arange(64)
    ang = 2 * np.pi * (np.outer(c, c) % 64) / 64
    for k, m in enumerate((np.cos(ang), np.sin(ang))):
        for g in range(2):
            tab[64 * g:64 * g + 64, C_CHAN + 128 * k + 64 * g:C_CHAN + 128 * k + 64 * g + 64] = m
    inv = (np.float32(10000.0) ** (-np.arange(32, dtype=np.float32) / np.float32(32))).astype(np.float32)
    tab[:, C_INVF:C_INVF + 32] = inv
    return tab.astype(np.float32)


_INS = ["x", "c", "positions", "w_ada", "b_ada", "w_in", "b_in", "w_fourier", "w_out", "b_out", "ln1_gain",
        "ln1_bias", "w_peer_q", "peer_subkeys", "peer_u", "peer_v", "ln2_gain", "ln2_bias"]


def kernel(**inputs):
    import concourse.bacc as bacc
    from concourse.bass_utils import run_bass_kernel_spmd

    nc = bacc.Bacc("TRN2", target_bir_lowering=False, num_devices=1)
    arrays, args = {}, []
    for name in _INS:
        a = np.ascontiguousarray(inputs[name])
        arrays[f"in_{name}"] = a
        args.append(nc.dram_tensor(f"in_{name}", a.shape, mybir.dt.from_np(a.dtype), kind="ExternalInput").ap())
    tab = constant_table()
    arrays["in_table"] = tab
    args.append(nc.dram_tensor("in_table", tab.shape, mybir.dt.float32, kind="ExternalInput").ap())
    out = nc.dram_tensor("out_0", (1, S, D), mybir.dt.float32, kind="ExternalOutput").ap()
    peer_encoder(nc, *args, out)
    r = run_bass_kernel_spmd(nc, [arrays], core_ids=[0])
    return r.results[0]["out_0"]
```
